# Optimizing a Trainium2 kernel written in Bass

```python
import jax, jax.numpy as jnp
from jax import lax
import numpy as np

D_MODEL = 1024
BATCH = 1
SEQ = 256
DEPTH = 2
DEC_BATCH = 8
DEC_SEQ = 8
PAST_LEN = 2048
PAGE_SIZE = 128

GLA_HEADS = 4
GLA_DK = 64
GLA_DV = 128
GLA_RANK = 16
GLA_TAU = 16.0
GLA_CHUNK = 64
SB_HEADS = 4
SB_DIM = 64
SB_BLOCK = 128
SB_BIAS_INIT = -8.0
CONV_CH = 256
CONV_WIDTH = 31
D_FF = 2816
EPS = 1e-6

GLA_QK = GLA_HEADS * GLA_DK
GLA_V = GLA_HEADS * GLA_DV
SB_W = SB_HEADS * SB_DIM
MIX_WIDTH = GLA_V + SB_W + CONV_CH
IN_SIZES = (GLA_QK, GLA_QK, GLA_V, GLA_V, GLA_RANK, SB_W, SB_W, SB_W, 2 * CONV_CH)
IN_COLS = sum(IN_SIZES)

kernel_name = "hymba_gla_stickbreak_conformer_macaron_step"

def rms_norm(x, g):
    xf = x.astype(jnp.float32)
    y = xf * lax.rsqrt(jnp.mean(xf * xf, axis=-1, keepdims=True) + EPS)
    return (y * g.astype(jnp.float32)).astype(x.dtype)

def layer_norm(x, g, b):
    xf = x.astype(jnp.float32)
    mu = jnp.mean(xf, axis=-1, keepdims=True)
    xc = xf - mu
    y = xc * lax.rsqrt(jnp.mean(xc * xc, axis=-1, keepdims=True) + EPS)
    return (y * g.astype(jnp.float32) + b.astype(jnp.float32)).astype(x.dtype)

def half_ffn(x, g_pre, g_post, w_gate, w_up, w_down):
    h = rms_norm(x, g_pre)
    f = (jax.nn.silu(h @ w_gate) * (h @ w_up)) @ w_down
    return x + 0.5 * rms_norm(f, g_post)

def gla_chunked(q, k, v, log_a, s0):
    B, T, H, dk = q.shape
    dv = v.shape[-1]
    C = min(GLA_CHUNK, T)
    n = -(-T // C)
    pad = n * C - T
    padt = lambda a: jnp.pad(a.astype(jnp.float32), ((0, 0), (0, pad), (0, 0), (0, 0)))
    to_chunks = lambda a: padt(a).reshape(B, n, C, H, a.shape[-1]).transpose(1, 0, 3, 2, 4)
    qs, ks, vs, as_ = to_chunks(q), to_chunks(k), to_chunks(v), to_chunks(log_a)
    tri = jnp.tril(jnp.ones((C, C), dtype=bool))

    def step(S, inp):
        qc, kc, vc, ac = inp
        b = jnp.cumsum(ac, axis=2)
        o_inter = jnp.einsum('bhtk,bhkv->bhtv', qc * jnp.exp(b), S)
        diff = b[:, :, :, None, :] - b[:, :, None, :, :]
        decay = jnp.exp(jnp.where(tri[:, :, None], diff, -jnp.inf))
        attn = jnp.einsum('bhtk,bhsk,bhtsk->bhts', qc, kc, decay)
        o = o_inter + jnp.einsum('bhts,bhsv->bhtv', attn, vc)
        b_last = b[:, :, -1:, :]
        S_new = jnp.exp(b_last[:, :, 0, :])[..., None] * S + jnp.einsum(
            'bhsk,bhsv->bhkv', kc * jnp.exp(b_last - b), vc)
        return S_new, o

    S, o = lax.scan(step, s0.astype(jnp.float32), (qs, ks, vs, as_))
    o = o.transpose(1, 0, 3, 2, 4).reshape(B, n * C, H, dv)[:, :T]
    return o, S

def stick_breaking(q, k, v, bias, q_pos, k_pos):
    B, Tq, H, d = q.shape
    qb = min(SB_BLOCK, Tq)
    nb = -(-Tq // qb)
    pad = nb * qb - Tq
    q = jnp.pad(q, ((0, 0), (0, pad), (0, 0), (0, 0)))
    q_pos = jnp.pad(q_pos, (0, pad), constant_values=-1)
    qs = q.reshape(B, nb, qb, H, d).transpose(1, 0, 2, 3, 4)
    ps = q_pos.reshape(nb, qb)
    scale = d ** -0.5
    kf = k.astype(jnp.float32)
    vf = v.astype(jnp.float32)
    bf = bias.astype(jnp.float32)[None, :, None, None]

    def block(args):
        qblk, pblk = args
        z = jnp.einsum('bqhd,bkhd->bhqk', qblk.astype(jnp.float32), kf) * scale + bf
        mask = (k_pos[None, :] < pblk[:, None])[None, None]
        log_1mb = jnp.where(mask, jax.nn.log_sigmoid(-z), 0.0)
        tail = lax.cumsum(log_1mb, axis=3, reverse=True) - log_1mb
        w = jnp.where(mask, jnp.exp(jax.nn.log_sigmoid(z) + tail), 0.0)
        return jnp.einsum('bhqk,bkhd->bqhd', w, vf)

    out = lax.map(block, (qs, ps))
    out = out.transpose(1, 0, 2, 3, 4).reshape(B, nb * qb, H, d)[:, :Tq]
    return out

def causal_dwconv(u, buf, w, b):
    C = u.shape[-1]
    full = jnp.concatenate([buf.astype(u.dtype), u], axis=1)
    y = lax.conv_general_dilated(full, w[:, None, :].astype(u.dtype), window_strides=(1,), padding='VALID',
                                 dimension_numbers=('NWC', 'WIO', 'NWC'), feature_group_count=C)
    return y + b, full[:, -(CONV_WIDTH - 1):]

def mixer(h, past_k, past_v, s0, buf, past_len, p):
    B, T, _ = h.shape
    z = h @ p['w_in']
    offs = np.cumsum(IN_SIZES)[:-1].tolist()
    gq, gk, gv, gg, glr, sq, sk, sv, cu = jnp.split(z, offs, axis=-1)
    q = gq.reshape(B, T, GLA_HEADS, GLA_DK) * (GLA_DK ** -0.5)
    k = gk.reshape(B, T, GLA_HEADS, GLA_DK)
    v = gv.reshape(B, T, GLA_HEADS, GLA_DV)
    log_a = (jax.nn.log_sigmoid((glr @ p['gla_w_a2'] + p['gla_b_a']).astype(jnp.float32)) / GLA_TAU)
    log_a = log_a.reshape(B, T, GLA_HEADS, GLA_DK)
    o_gla, s_new = gla_chunked(q, k, v, log_a, s0)
    o_gla = rms_norm(o_gla, p['gla_norm'].reshape(GLA_HEADS, GLA_DV)).reshape(B, T, GLA_V)
    o_gla = (o_gla * jax.nn.silu(gg.astype(jnp.float32))).astype(h.dtype)
    q_sb = sq.reshape(B, T, SB_HEADS, SB_DIM)
    k_new = sk.reshape(B, T, SB_HEADS, SB_DIM)
    v_new = sv.reshape(B, T, SB_HEADS, SB_DIM)
    k_all = jnp.concatenate([past_k.astype(k_new.dtype), k_new], axis=1)
    v_all = jnp.concatenate([past_v.astype(v_new.dtype), v_new], axis=1)
    q_pos = past_len + jnp.arange(T, dtype=jnp.int32)
    k_pos = jnp.arange(past_len + T, dtype=jnp.int32)
    o_sb = stick_breaking(q_sb, k_all, v_all, p['sb_bias'], q_pos, k_pos).reshape(B, T, SB_W).astype(h.dtype)
    a, gate = jnp.split(cu, 2, axis=-1)
    u = a * jax.nn.sigmoid(gate)
    y, buf_new = causal_dwconv(u, buf, p['conv_w'], p['conv_b'])
    y = jax.nn.silu(layer_norm(y, p['conv_norm_g'], p['conv_norm_b'])).astype(h.dtype)
    mix = jnp.concatenate([o_gla, o_sb, y], axis=-1)
    return mix @ p['w_out'], k_new, v_new, s_new, buf_new

def decoder_layer(x, past_k, past_v, s0, buf, past_len, p):
    x = half_ffn(x, p['ffn1_norm_pre'], p['ffn1_norm_post'], p['ffn1_w_gate'], p['ffn1_w_up'], p['ffn1_w_down'])
    m, k_new, v_new, s_new, buf_new = mixer(rms_norm(x, p['mix_norm_pre']), past_k, past_v, s0, buf, past_len, p)
    x = x + rms_norm(m, p['mix_norm_post'])
    x = half_ffn(x, p['ffn2_norm_pre'], p['ffn2_norm_post'], p['ffn2_w_gate'], p['ffn2_w_up'], p['ffn2_w_down'])
    return x, k_new, v_new, s_new, buf_new

def setup_inputs(seed: int = 0) -> dict:
    key = jax.random.key(seed)
    keys = jax.random.split(key, 32)
    f32 = jnp.float32
    nrm = lambda i, shape, scale: jax.random.normal(keys[i], shape, f32) * scale
    gain = lambda i, shape: 1.0 + 0.02 * jax.random.normal(keys[i], shape, f32)
    n_pages = PAST_LEN // PAGE_SIZE
    n_used = DEC_BATCH * n_pages
    n_pool = n_used + (n_used + 3) // 4
    page_table = jax.random.permutation(keys[4], n_pool)[:n_used].reshape(DEC_BATCH, n_pages).astype(jnp.int32)
    L, D, F = DEPTH, D_MODEL, D_FF
    return {
        'x_prompt': nrm(0, (BATCH, SEQ, D), 1.0),
        'x_sample': nrm(1, (DEC_BATCH, DEC_SEQ, D), 1.0),
        'cache_sb_k': nrm(2, (L, n_pool, PAGE_SIZE, SB_HEADS, SB_DIM), 1.0),
        'cache_sb_v': nrm(3, (L, n_pool, PAGE_SIZE, SB_HEADS, SB_DIM), 1.0),
        'page_table': page_table,
        'state_gla': nrm(5, (L, DEC_BATCH, GLA_HEADS, GLA_DK, GLA_DV), 1.0),
        'state_conv': nrm(6, (L, DEC_BATCH, CONV_WIDTH - 1, CONV_CH), 0.5),
        'ffn1_norm_pre': gain(7, (L, D)),
        'ffn1_norm_post': gain(8, (L, D)),
        'ffn1_w_gate': nrm(9, (L, D, F), D ** -0.5),
        'ffn1_w_up': nrm(10, (L, D, F), D ** -0.5),
        'ffn1_w_down': nrm(11, (L, F, D), F ** -0.5),
        'mix_norm_pre': gain(12, (L, D)),
        'mix_norm_post': gain(13, (L, D)),
        'w_in': nrm(14, (L, D, IN_COLS), D ** -0.5),
        'gla_w_a2': nrm(15, (L, GLA_RANK, GLA_QK), GLA_RANK ** -0.5),
        'gla_b_a': nrm(16, (L, GLA_QK), 0.1),
        'gla_norm': gain(17, (L, GLA_V)),
        'sb_bias': SB_BIAS_INIT + nrm(28, (L, SB_HEADS), 0.1),
        'conv_w': nrm(18, (L, CONV_WIDTH, CONV_CH), CONV_WIDTH ** -0.5),
        'conv_b': nrm(19, (L, CONV_CH), 0.02),
        'conv_norm_g': gain(20, (L, CONV_CH)),
        'conv_norm_b': nrm(21, (L, CONV_CH), 0.02),
        'w_out': nrm(22, (L, MIX_WIDTH, D), MIX_WIDTH ** -0.5),
        'ffn2_norm_pre': gain(23, (L, D)),
        'ffn2_norm_post': gain(24, (L, D)),
        'ffn2_w_gate': nrm(25, (L, D, F), D ** -0.5),
        'ffn2_w_up': nrm(26, (L, D, F), D ** -0.5),
        'ffn2_w_down': nrm(27, (L, F, D), F ** -0.5),
    }

def reference(x_prompt, x_sample, cache_sb_k, cache_sb_v, page_table, state_gla, state_conv,
              ffn1_norm_pre, ffn1_norm_post, ffn1_w_gate, ffn1_w_up, ffn1_w_down,
              mix_norm_pre, mix_norm_post, w_in, gla_w_a2, gla_b_a, gla_norm, sb_bias,
              conv_w, conv_b, conv_norm_g, conv_norm_b, w_out,
              ffn2_norm_pre, ffn2_norm_post, ffn2_w_gate, ffn2_w_up, ffn2_w_down):
    past_len = page_table.shape[1] * cache_sb_k.shape[2]
    B = x_prompt.shape[0]
    DB = x_sample.shape[0]
    xp, xs = x_prompt, x_sample
    pk, pv, ps, pc, sk, sv, ss, sc = [], [], [], [], [], [], [], []
    for l in range(DEPTH):
        p = dict(ffn1_norm_pre=ffn1_norm_pre[l], ffn1_norm_post=ffn1_norm_post[l], ffn1_w_gate=ffn1_w_gate[l],
                 ffn1_w_up=ffn1_w_up[l], ffn1_w_down=ffn1_w_down[l], mix_norm_pre=mix_norm_pre[l],
                 mix_norm_post=mix_norm_post[l], w_in=w_in[l], gla_w_a2=gla_w_a2[l], gla_b_a=gla_b_a[l],
                 gla_norm=gla_norm[l], sb_bias=sb_bias[l], conv_w=conv_w[l], conv_b=conv_b[l],
                 conv_norm_g=conv_norm_g[l], conv_norm_b=conv_norm_b[l], w_out=w_out[l],
                 ffn2_norm_pre=ffn2_norm_pre[l], ffn2_norm_post=ffn2_norm_post[l],
                 ffn2_w_gate=ffn2_w_gate[l], ffn2_w_up=ffn2_w_up[l], ffn2_w_down=ffn2_w_down[l])
        empty = jnp.zeros((B, 0, SB_HEADS, SB_DIM), xp.dtype)
        s0 = jnp.zeros((B, GLA_HEADS, GLA_DK, GLA_DV), jnp.float32)
        buf0 = jnp.zeros((B, CONV_WIDTH - 1, CONV_CH), xp.dtype)
        xp, k1, v1, s1, c1 = decoder_layer(xp, empty, empty, s0, buf0, 0, p)
        pk.append(k1); pv.append(v1); ps.append(s1); pc.append(c1)
        past_k = cache_sb_k[l][page_table].reshape(DB, past_len, SB_HEADS, SB_DIM)
        past_v = cache_sb_v[l][page_table].reshape(DB, past_len, SB_HEADS, SB_DIM)
        xs, k2, v2, s2, c2 = decoder_layer(xs, past_k, past_v, state_gla[l], state_conv[l], past_len, p)
        sk.append(k2); sv.append(v2); ss.append(s2); sc.append(c2)
    return (xp, xs, jnp.stack(pk), jnp.stack(pv), jnp.stack(ps), jnp.stack(pc),
            jnp.stack(sk), jnp.stack(sv), jnp.stack(ss), jnp.stack(sc))


_drawn_inputs = setup_inputs


def setup_inputs(seed=0):
    import zlib

    import numpy as np

    out = dict(_drawn_inputs(seed))
    spreads = {}
    factors = {'ffn1_norm_post': 2.881,
     'gla_norm': 14.361,
     'sb_bias': 8.0,
     'conv_norm_g': 16.857,
     'conv_norm_b': 16.859,
     'ffn2_norm_pre': 3.912,
     'ffn2_norm_post': 16.243,
     'mix_norm_post': 3.111}
    for name, (base, spread) in spreads.items():
        noise = np.random.default_rng([zlib.crc32(name.encode()), seed]).standard_normal(out[name].shape)
        drawn = base * np.exp(spread * noise) if base else spread * noise
        out[name] = __import__('jax').numpy.asarray(drawn.astype(out[name].dtype))
    for name, factor in factors.items():
        out[name] = (out[name] * factor).astype(out[name].dtype)
    return out
```

```python
from contextlib import ExitStack, contextmanager

import numpy as np

import concourse.bass as bass
from concourse import mybir

ALU = mybir.AluOpType
ACT = mybir.ActivationFunctionType
F32 = mybir.dt.float32
F32R = mybir.dt.float32r
U8 = mybir.dt.uint8
I32 = mybir.dt.int32

P = 128
D = 1024
F = 2816
KD = D // P
FT = F // P
L = 2
TP = 256
DB, DT = 8, 8
TS = DB * DT
T = TP + TS
TPAD = 384
NT = 3
G = 4
PAGES = 16
H = 4
DK = 64
DV = 128
TAPS = 31
HALO = TAPS - 1
EXT = HALO + TP + DB * (HALO + DT)
EPS = 1e-6
NEG = -1e30
SLOTS = 4
LEAD = 4
DOWN = ((0, 8), (8, 7), (15, 7))
LEVELS = (1, 2, 4, 8, 16, 32, 64)

UNITS_IN = ([("a", 0, 2320), ("g", 0, 2576), ("a", 1, 2448), ("g", 1, 2704)]
            + [("gg", c, 1024 + P * c) for c in range(4)] + [("glr", 0, 1536)]
            + [("gq", c, P * c) for c in range(2)] + [("gk", c, 256 + P * c) for c in range(2)]
            + [("gv", c, 512 + P * c) for c in range(4)]
            + [("sq", c, 1552 + P * c) for c in range(2)] + [("sk", c, 1808 + P * c) for c in range(2)]
            + [("sv", c, 2064 + P * c) for c in range(2)])
ON_ACT = ("g", "gg", "glr", "gq", "sq", "sk")
NIN = len(UNITS_IN)
U_FFN = 2 * FT + 3 * KD
U_IN = U_FFN
U_OUT = U_IN + NIN
U_FFN2 = U_OUT + KD
U_END = U_FFN2 + U_FFN

PAR = {}
_n = 0
for _name, _rows in (("ffn1_norm_pre", 8), ("mix_norm_pre", 8), ("ffn2_norm_pre", 8), ("ffn1_norm_post", 8),
                     ("mix_norm_post", 8), ("ffn2_norm_post", 8), ("gla_b_a", 2), ("gla_norm", 4), ("conv_b", 2),
                     ("conv_norm_g", 2), ("conv_norm_b", 2), ("conv_w", 2 * TAPS)):
    PAR[_name] = _n
    _n += _rows
NPAR = _n


def constants():
    i = np.arange(P)
    parts, at, n = [], {}, 0

    def put(name, a):
        nonlocal n
        full = np.zeros((P, a.shape[1]), np.float32)
        full[:a.shape[0]] = a
        at[name] = (n, n + a.shape[1])
        n += a.shape[1]
        parts.append(full)

    put("ident", np.eye(P))
    put("mean_d", np.full((P, P), 1.0 / D))
    put("mean_dv", np.full((P, P), 1.0 / DV))
    put("mean_ch", np.full((P, P), 1.0 / 256))
    put("ones", np.ones((P, P)))
    put("from_here", (i[:, None] >= i[None, :]).astype(np.float32))
    seg = np.ones(T)
    seg[[0, P]] = 0
    seg[TP::DT] = 0
    put("gla_keep", np.tile(seg, (P, 1)))
    put("causal", np.where(i[:, None] < i[None, :], 0, NEG))
    b, t = i[:TS] // DT, i[:TS] % DT
    qbatch, qhead, qt_ = i // 32, i // DT % H, i % DT
    mask = [np.where((b[None, :] == G * g + qbatch[:, None]) & (t[None, :] < qt_[:, None]), 0, NEG) for g in range(DB // G)]
    put("new_mask", np.concatenate(mask, 1))
    put("head_of", (qhead[:, None] == np.arange(H)[None, :]).astype(np.float32))
    put("batch_of", (b[:, None] == np.arange(DB)[None, :]).astype(np.float32))
    put("eps", np.full((P, 1), EPS))
    level = np.zeros((P, 8, P), np.int32)
    level[:, 0] = np.eye(P)
    for n_, w in enumerate(LEVELS):
        s, q = i[:, None], i[None, :]
        level[:, n_ + 1] = (s // (2 * w) == q // (2 * w)) & (s % (2 * w) < w) & (q % (2 * w) >= w)
    return np.concatenate(parts, 1), at, level.reshape(P, 8 * P)


CONST, AT, LEVEL = constants()


SEMAPHORES = """
const_loaded x_loaded x_stored x_turned x_placed par_loaded state_loaded state_out
w_loaded0 w_loaded1 w_loaded2 w_loaded3 w_hi w_lo w_used act_step dve_step par_turned par_ready half_ready
sq_ready sq_used r_ready h_ready h_hi h_lo x_ready gate_act gate_up gu_hi gu_lo f_ready fsq_ready ss_done post_mean
zin_act zin_dve qb_clear cst_turned cst_placed out_turned out_placed_act out_placed_dve
loga_pre loga_x loga_neg loga_l b_ready qk_d qk_e qk_ready qk_used att_done khat_d khat_e khat_ready
knat_turned knat_ready knm_ready s1_prod st_prod s1_ready s2_ready st_done o_prod o_sq o_mean o_r o_done
conv_packed conv_y conv_mean conv_d conv_v conv_var conv_r conv_n conv_done
qb_ready pz_prod pz_neg pz_l pz_sp pz_cum pz_lw pz_w po_done
zn_prod zn_neg zn_l zn_lw wn_ready
zn_s wn_turned wn_placed
k_loaded0 k_loaded1 v_loaded0 v_loaded1 kt_turned kt_act kt_dve kt_used z_placed z_l lw_ready w_ready wt_turned wt_placed v_used
po_prod oq_placed oq_turned so_done mix_hi mix_lo y_turned y_placed
"""


class Steps:

    def __init__(self, eng, own):
        self.eng, self.own, self.count, self.last = eng, own, {}, None
        self.per, self.turn = {}, 0

    def __call__(self, ins, sem=None):
        sem = self.own if sem is None else sem
        ins.then_inc(sem, 1)
        self.count[sem.name] = self.count.get(sem.name, 0) + 1
        self.last = (sem, self.count[sem.name])
        return ins

    def settle(self):
        sem, n = self.last
        per = self.per.get(sem.name, 0)
        self.eng.wait_ge(sem, self.turn * per + n if per else n)

    @contextmanager
    def repeat(self, start, stop, per):
        before = dict(self.count)
        self.per = {s.name: k for s, k in per}
        with self.eng.Fori(start, stop) as i:
            self.turn = i - start
            yield i
        for name, n in self.count.items():
            if n != before.get(name, 0):
                assert n - before.get(name, 0) == self.per.get(name), (name, n, before.get(name), self.per.get(name))
                self.count[name] = before.get(name, 0) + self.per[name] * (stop - start)
        self.last = (self.last[0], self.count[self.last[0].name])
        self.per, self.turn = {}, 0


def build(nc, ins, outs):
    stack = ExitStack()
    top = [nc.sbuf_base + 31 & ~31]

    def sb(name, shape, dt=F32, at=None):
        size = int(np.prod(shape[1:])) * (1 if dt == U8 else 4)
        size = size + 31 & ~31
        where = top[0] if at is None else at[0]
        if at is None:
            top[0] += size
        else:
            at[0] += size
        return nc.alloc_sbuf_tensor_at(name, shape, dt, offset=where)

    sems = []

    def sem(name):
        s = stack.enter_context(nc.semaphore(name))
        sems.append(s)
        return s

    const = sb("const", [P, CONST.shape[1]])
    level = sb("level", [P, 8, P], U8)
    xT = sb("xT", [P, KD, T])
    raw = sb("raw", [P, SLOTS, 8, P])
    w_h = sb("w_h", [P, SLOTS, 8, P], F32R)
    w_l = sb("w_l", [P, SLOTS, 8, P], F32R)
    h_at = top[0]
    hh = sb("hh", [P, KD, TPAD], F32R)
    hl = sb("hl", [P, KD, TPAD], F32R)
    h_end = top[0]
    fT = sb("fT", [P, KD, T])
    sq = sb("sq", [P, 2, T])
    ss = sb("ss", [P, T])
    rs = sb("rs", [P, T])
    rln = sb("rln", [P, T])
    ht = sb("ht", [P, 2, T])
    parn = sb("parn", [P, P])
    par = sb("par", [P, NPAR])
    sbb = sb("sbb", [P, H])
    wa2 = sb("wa2", [16, 256])
    pages = sb("pages", [1, DB * PAGES], I32)
    base = top[0]
    a = [base]
    guh = sb("guh", [P, FT, T], F32R, a)
    gul = sb("gul", [P, FT, T], F32R, a)
    sg = sb("sg", [P, 2, T], at=a)
    gt = sb("gt", [P, 2, T], at=a)
    end_ffn = a[0]
    a = [base]
    qs = sb("qs", [P, 2, T], at=a)
    ks = sb("ks", [P, 2, T], at=a)
    svn = sb("svn", [P, NT, 256], at=a)
    yT = sb("yT", [P, 2, T], at=a)
    ext = sb("ext", [P, 2, EXT], at=a)
    qb = sb("qb", [P, 2, DB * 32], at=a)
    bq = sb("bq", [P, 1], at=a)
    zn = sb("zn", [P, DB // G, TS], at=a)
    tn = sb("tn", [P, DB // G, TS], at=a)
    sn = sb("sn", [P, DB // G, TS], at=a)
    wTn = sb("wTn", [P, DB // G, P], at=a)
    both = a[0]
    gate = sb("gate", [P, 4, T], at=a)
    gq = sb("gq", [P, 2, T], at=a)
    gk = sb("gk", [P, 2, T], at=a)
    gv = sb("gv", [P, NT, 512], at=a)
    glr = sb("glr", [16, T], at=a)
    st = sb("st", [P, DB, 2, DV], at=a)
    bb = sb("bb", [P, 2, T], at=a)
    dd = sb("dd", [P, 2, 2, T], at=a)
    qt = sb("qt", [P, 2, 2, T], at=a)
    kt = sb("kt", [P, 2, 2, T], at=a)
    att = sb("att", [P, NT, H, P], at=a)
    kn = sb("kn", [P, NT, 256], at=a)
    knm = sb("knm", [TS, DB, 256], at=a)
    aend = sb("aend", [P, 2, 10], at=a)
    s1 = sb("s1", [P, 2, DV], at=a)
    s2 = sb("s2", [P, 2, DV], at=a)
    osq = sb("osq", [P, H, T], at=a)
    end_gla = a[0]
    cst = sb("cst", [P, 2, 256], at=a)
    skn = sb("skn", [P, NT, 256], at=a)
    cso = sb("cso", [P, 3, 256], at=a)
    end_a = a[0]
    a = [both]
    ps_z = sb("ps_z", [P, 3, 512], at=a)
    ps_t = sb("ps_t", [P, 3, 512], at=a)
    ps_s = sb("ps_s", [P, 3, 512], at=a)
    vpg = sb("vpg", [P, 2, G, 4, 256], at=a)
    kT = sb("kT", [P, 2, G, 2, 256], at=a)
    z_ = sb("z_", [P, 2, 512], at=a)
    t_ = sb("t_", [P, 2, 512], at=a)
    s_ = sb("s_", [P, 2, 512], at=a)
    oq = ht[:, 0, 0:256]
    end_s = a[0]
    a = [h_at]
    kpg = sb("kpg", [P, 2, G, 2, 256], at=a)
    w_ = sb("w_", [P, 2, 512], at=a)
    wT = sb("wT", [P, 2, 4, P], at=a)
    assert a[0] <= h_end
    nc_end = max(end_ffn, end_a, end_s)
    assert nc_end <= nc.sbuf_usable_end, (nc_end, nc.sbuf_usable_end, end_ffn, end_a, end_s)
    xn = nc.alloc_sbuf_tensor_at("xn", [P, NT, D], F32, offset=base)
    level_in = nc.alloc_sbuf_tensor_at("level_in", [P, 8 * P], I32, offset=base + NT * D * 4)

    def cst_(name, rows=P, cols=None):
        lo, hi = AT[name]
        return const[0:rows, lo:hi if cols is None else lo + cols]

    bank = [stack.enter_context(nc.psum_tensor(f"bank{i}", [P, 512], F32)) for i in range(8)]
    sm = {name: sem(name) for name in SEMAPHORES.split()}
    w_loaded = [sm[f"w_loaded{s}"] for s in range(SLOTS)]
    k_loaded = [sm["k_loaded0"], sm["k_loaded1"]]
    v_loaded = [sm["v_loaded0"], sm["v_loaded1"]]

    with nc.Block() as block:
        @block.sync
        def _(sp_):
            sp_.dma_start(const[:, :], ins["const"]).then_inc(sm["const_loaded"], 16)
            sp_.dma_start(level_in[:, :], ins["level"]).then_inc(sm["const_loaded"], 16)
            sp_.dma_start(pages[:, :], ins["page_table"].rearrange("(o b) n -> o (b n)", o=1)).then_inc(sm["const_loaded"], 16)
            sp_.dma_start(xn[:, 0:2, :], ins["x_prompt"].rearrange("o (n p) d -> p (o n) d", p=P)).then_inc(sm["x_loaded"], 16)
            sp_.dma_start(xn[0:TS, 2, :], ins["x_sample"].rearrange("b t d -> (b t) d")).then_inc(sm["x_loaded"], 16)

        @block.tensor
        def _(pe):
            pe.wait_ge(sm["const_loaded"], 48)
            pe.wait_ge(sm["x_loaded"], 32)
            for j in range(KD):
                if j >= 4:
                    pe.wait_ge(sm["x_placed"], j - 3)
                for n in range(NT):
                    rows = P if n < 2 else TS
                    ins_ = pe.transpose(bank[j % 4][:, n * P:n * P + rows], xn[0:rows, n, j * P:(j + 1) * P],
                                        cst_("ident", rows, rows))
                ins_.then_inc(sm["x_turned"], 1)

        @block.vector
        def _(dve):
            dve.memset(hh[:, :, :].bitcast(I32), 0)
            dve.memset(hl[:, :, :].bitcast(I32), 0)
            dve.wait_ge(sm["const_loaded"], 48)
            dve.tensor_copy(level[:, :, :].rearrange("p a b -> p (a b)"), level_in[:, :])
            for j in range(KD):
                dve.wait_ge(sm["x_turned"], j + 1)
                dve.tensor_copy(xT[:, j, :], bank[j % 4][:, 0:T]).then_inc(sm["x_placed"], 1)
    def clear():
        for s in sems:
            nc.sync.sem_clear(s)
        nc.all_engine_barrier()

    clear()

    with nc.Fori(0, L) as layer:
        one = bass.ds(layer, 1)

        def lay(ap, pattern, **kw):
            letters = pattern.split("->")
            return ap[one].rearrange("l " + letters[0] + "->" + letters[1].replace("*", "l"), **kw)

        def load_page(eng, dst, cache, it, b, n, loaded, free=None):
            at = (it // (PAGES // 4) * G + b) * PAGES + first_page(it) + n
            idx = eng.value_load(pages[0:1, at:at + 1], min_val=0, max_val=cache.shape[1] - 1)
            if free is not None:
                eng.wait_ge(*free)
            eng.dma_start(dst.rearrange("p (h d) -> p h d", h=H), cache[one, bass.ds(idx, 1)].rearrange("l n p h d -> p (l n h) d")).then_inc(loaded, 16)

        with nc.Block() as block:
            @block.sync
            def _(sp_):
                def load(u, src, n, static=True, first=False):
                    slot = (u if isinstance(u, int) else u[0]) % SLOTS
                    if isinstance(u, int):
                        if u >= SLOTS:
                            sp_.wait_ge(sm["w_lo"], u - SLOTS + 1)
                    else:
                        sp_.wait_ge(sm["w_lo"], u[1] + (u[0] - SLOTS + 1))
                    sp_.dma_start(raw[:, slot, 0:n, :], src).then_inc(w_loaded[slot], 16)

                def cols(w, k0, n, c):
                    src = w[one, k0 * P:(k0 + n) * P, c if isinstance(c, bass.DynSlice) else slice(c, c + P)]
                    return src.rearrange("l (k p) f -> p (l k) f", p=P)

                def ffn(U0, wg, wu, wd):
                    def pair(i, u):
                        for t in range(2):
                            c = bass.ds((2 * i + t) * P, P)
                            for m, w in ((0, wg), (1, wu)):
                                load(u(2 * t + m), cols(w, 0, KD, c), KD)
                    pair(0, lambda j: U0 + j)
                    with sp_.Fori(1, FT // 2) as i:
                        pair(i, lambda j: (U0 + j, i * 4))
                    Ud = U0 + 2 * FT

                    def four(i, u):
                        for n in range(4):
                            for m, (k0, kn_) in enumerate(DOWN):
                                load(u(3 * n + m), cols(wd, k0, kn_, bass.ds((4 * i + n) * P, P)), kn_)
                    with sp_.Fori(0, 2) as i:
                        four(i, lambda j: (Ud + j, i * 12))

                ffn(0, ins["ffn1_w_gate"], ins["ffn1_w_up"], ins["ffn1_w_down"])
                for m, (_, _, c) in enumerate(UNITS_IN):
                    load(U_IN + m, cols(ins["w_in"], 0, KD, c), KD)
                for n in range(LEAD):
                    load(U_OUT + n, cols(ins["w_out"], 0, KD, n * P), KD)

                sp_.wait_ge(sm["w_used"], U_OUT)
                for it in range(ITS):
                    for s_i in range(2):
                        for b in range(G):
                            for j in range(2):
                                load_page(sp_, kpg[:, s_i, b, j, :], ins["cache_sb_k"], it, b, 2 * s_i + j, k_loaded[s_i],
                                          (sm["kt_turned"], 8 * it - 4 + 4 * s_i) if it and b == j == 0 else None)
                for n in range(LEAD, KD):
                    load(U_OUT + n, cols(ins["w_out"], 0, KD, n * P), KD)
                ffn(U_FFN2, ins["ffn2_w_gate"], ins["ffn2_w_up"], ins["ffn2_w_down"])

            @block.gpsimd
            def _(pool):
                n = 0
                for name in ("ffn1_norm_pre", "mix_norm_pre", "ffn2_norm_pre", "ffn1_norm_post", "mix_norm_post",
                             "ffn2_norm_post", "gla_b_a", "gla_norm", "conv_b", "conv_norm_g", "conv_norm_b"):
                    rows = ins[name].shape[1] // P
                    pool.dma_start(parn[PAR[name]:PAR[name] + rows, :],
                                   ins[name][one].rearrange("l (r c) -> (l r) c", c=P)).then_inc(sm["par_loaded"], 16)
                pool.dma_start(parn[PAR["conv_w"]:PAR["conv_w"] + 2 * TAPS, :],
                               ins["conv_w"][one].rearrange("l k (r c) -> (l k r) c", c=P)).then_inc(sm["par_loaded"], 16)
                pool.dma_start(wa2[:, :], ins["gla_w_a2"][one].rearrange("l r c -> (l r) c")).then_inc(sm["par_loaded"], 16)
                pool.dma_start(sbb[:, :], ins["sb_bias"][one].to_broadcast([P, H])).then_inc(sm["par_loaded"], 16)
                pool.wait_ge(sm["w_used"], U_IN)
                for p_ in range(2):
                    pool.dma_start(st[:, :, p_, :], ins["state_gla"][one, :, 2 * p_:2 * p_ + 2].rearrange("l b h k v -> (h k) (l b) v")).then_inc(sm["state_loaded"], 16)
                for g in range(2):
                    pool.dma_start(cst[0:4 * HALO, g, :], ins["state_conv"][one, 4 * g:4 * g + 4].rearrange("l b k c -> (l b k) c")).then_inc(sm["state_loaded"], 16)
                pool.wait_ge(sm["out_placed_act"], 2)
                pool.wait_ge(sm["out_placed_dve"], 2)
                pool.wait_ge(sm["zin_dve"], sum(1 for k in UNITS_IN if k[0] not in ON_ACT))
                so = sm["state_out"]
                for name, t in (("k", skn), ("v", svn)):
                    pool.dma_start(outs["prompt_sb_" + name][one].rearrange("l o (n p) h d -> p (l o n) (h d)", p=P), t[:, 0:2, :]).then_inc(so, 16)
                    pool.dma_start(outs["sample_sb_" + name][one].rearrange("l b t h d -> (l b t) (h d)"), t[0:TS, 2, :]).then_inc(so, 16)
                pool.dma_start(outs["prompt_conv_state"][one].rearrange("l o k c -> (l o k) c"), cso[0:HALO, 2, :]).then_inc(so, 16)
                for g in range(2):
                    pool.dma_start(outs["sample_conv_state"][one, 4 * g:4 * g + 4].rearrange("l b k c -> (l b k) c"), cso[0:4 * HALO, g, :]).then_inc(so, 16)
                pool.wait_ge(sm["st_done"], 16)
                for p_ in range(2):
                    pool.dma_start(outs["sample_gla_state"][one, :, 2 * p_:2 * p_ + 2].rearrange("l b h k v -> (h k) (l b) v"), st[:, :, p_, :]).then_inc(so, 16)
                pool.wait_ge(sm["s2_ready"], 2)
                pool.dma_start(outs["prompt_gla_state"][one].rearrange("l o (p h) k v -> (h k) (l o p) v", p=2), s2[:, :, :]).then_inc(so, 16)
                pool.wait_ge(so, 16 * 10)
                pool.wait_ge(sm["pz_w"], 1)
                pool.wait_ge(sm["po_prod"], 1)
                for it in range(ITS):
                    for b in range(G):
                        for n in range(4):
                            load_page(pool, vpg[:, it % 2, b, n, :], ins["cache_sb_v"], it, b, n, v_loaded[it % 2],
                                      (sm["v_used"], it - 1) if it >= 2 and b == n == 0 else None)
                pool.wait_ge(sm["par_loaded"], 16 * 14)
                pool.wait_ge(sm["state_loaded"], 16 * 4)
                for v in v_loaded:
                    pool.wait_ge(v, 256 * ITS // 2)
                pool.dma_reset()

            @block.tensor
            def _(pe):
                def product(out, pairs, width=T, m=P):
                    last = None
                    for n, (lh, ll, rh, rl) in enumerate(pairs):
                        pe.matmul(out, lh, rh, start=(n == 0), stop=False)
                        pe.matmul(out, lh, rl, start=False, stop=False)
                        last = pe.matmul(out, ll, rh, start=False, stop=(n == len(pairs) - 1))
                    return last

                def unit(u, out, rhs_h, rhs_l, n, k0=0, tiles=KD, first_wait=None, c8=0):
                    slot = (u if isinstance(u, int) else u[0]) % SLOTS
                    pe.wait_ge(sm["w_lo"], u + 1 if isinstance(u, int) else u[1] + (u[0] + 1))
                    last = None
                    for k in range(n):
                        if first_wait is not None:
                            pe.wait_ge(first_wait, c8 + k + 1)
                        f, l_ = k0 + k == 0, k0 + k == tiles - 1
                        kk = k0 + k
                        pe.matmul(out, w_h[:, slot, k, :], rhs_h[:, kk, 0:T], start=f, stop=False)
                        pe.matmul(out, w_h[:, slot, k, :], rhs_l[:, kk, 0:T], start=False, stop=False)
                        last = pe.matmul(out, w_l[:, slot, k, :], rhs_h[:, kk, 0:T], start=False, stop=l_)
                    last.then_inc(sm["w_used"], 1)

                def pre_norm(c):
                    for j in range(KD):
                        pe.wait_ge(sm["sq_ready"], 8 * c + j + 1)
                        pe.matmul(bank[6][:, 0:T], cst_("mean_d"), sq[:, j % 2, :], start=(j == 0), stop=(j == KD - 1)).then_inc(sm["sq_used"], 1)

                def post_norm(c):
                    pe.wait_ge(sm["ss_done"], 8 * c + 8)
                    pe.matmul(bank[6][:, 0:T], cst_("mean_d"), ss[:, :], start=True, stop=True).then_inc(sm["post_mean"], 1)

                def ffn(k, U0):
                    c = 2 * k
                    pre_norm(c)

                    def pair(i, u, peeled):
                        for t in range(2):
                            done = (lambda s: pe.wait_ge(s, k * FT + 2 * i + t - 1)) if not peeled else (
                                (lambda s: pe.wait_ge(s, k * FT)) if k else (lambda s: None))
                            done(sm["gate_act"])
                            unit(u(2 * t), bank[2 * t][:, 0:T], hh, hl, KD,
                                 first_wait=sm["h_lo"] if peeled and t == 0 else None, c8=8 * c)
                            done(sm["gate_up"])
                            unit(u(2 * t + 1), bank[2 * t + 1][:, 0:T], hh, hl, KD)
                    pair(0, lambda j: U0 + j, True)
                    with pe.Fori(1, FT // 2) as i:
                        pair(i, lambda j: (U0 + j, i * 4), False)
                    Ud = U0 + 2 * FT
                    pe.wait_ge(sm["gu_lo"], (k + 1) * FT)

                    def four(i, u, peeled):
                        for n in range(4):
                            if not peeled or n >= 2:
                                pe.wait_ge(sm["f_ready"], 8 * c + n - 1 + (0 if peeled else 4 * i))
                            for m, (k0, kn_) in enumerate(DOWN):
                                unit(u(3 * n + m), bank[4 + n % 2][:, 0:T], guh, gul, kn_, k0, FT)
                    four(0, lambda j: Ud + j, True)
                    four(1, lambda j: Ud + 12 + j, False)
                    post_norm(c)

                pe.wait_ge(sm["par_loaded"], 16 * 14)
                pe.transpose(bank[7][:, 0:NPAR], parn[0:NPAR, :], cst_("ident", NPAR, NPAR)).then_inc(sm["par_turned"], 1)
                ffn(0, 0)

                pre_norm(1)
                pe.wait_ge(sm["state_loaded"], 64)
                for g in range(2):
                    for c in range(2):
                        last = pe.transpose(bank[7][:, (2 * g + c) * 120:(2 * g + c) * 120 + 120],
                                            cst[0:120, g, c * P:(c + 1) * P], cst_("ident", 120, 120))
                last.then_inc(sm["cst_turned"], 1)
                evac, n_act, n_dve = [], 0, 0
                for what, _, _ in UNITS_IN:
                    if what in ON_ACT:
                        n_act += 1
                        evac.append((sm["zin_act"], n_act))
                    else:
                        n_dve += 1
                        evac.append((sm["zin_dve"], n_dve))
                for m, (what, c, _) in enumerate(UNITS_IN):
                    if m >= 4:
                        pe.wait_ge(*evac[m - 4])
                    out = bank[m % 4]
                    if what not in ("gv", "sv"):
                        unit(U_IN + m, out[:, 0:T], hh, hl, KD, first_wait=sm["h_lo"] if m == 0 else None, c8=8)
                        continue
                    slot = (U_IN + m) % SLOTS
                    pe.wait_ge(sm["w_lo"], U_IN + m + 1)
                    for n in range(NT):
                        t_ = slice(n * P, (n + 1) * P)
                        last = product(out[:, t_], [(hh[:, k, t_], hl[:, k, t_], w_h[:, slot, k, :], w_l[:, slot, k, :])
                                                    for k in range(KD)])
                    last.then_inc(sm["w_used"], 1)

                pe.wait_ge(*evac[NIN - 1])
                pe.wait_ge(*evac[NIN - 3])
                for n in range(NT):
                    rows = P if n < 2 else TS
                    for c in range(2):
                        last = pe.transpose(bank[n // 2][0:rows, (n % 2) * 256 + c * P:(n % 2) * 256 + (c + 1) * P],
                                            ks[:, c, n * P:n * P + rows], cst_("ident"))
                last.then_inc(sm["out_turned"], 1)
                for c in range(2):
                    pe.wait_ge(sm["conv_packed"], c + 1)
                    for g in range(2):
                        pe.transpose(bank[2][0:120, (2 * g + c) * P:(2 * g + c + 1) * P], cst[:, c, g * 120:g * 120 + 120], cst_("ident"))
                    last = pe.transpose(bank[3][0:HALO, c * P:(c + 1) * P], ext[:, c, TP:TP + HALO], cst_("ident"))
                last.then_inc(sm["out_turned"], 1)

                for p_ in range(2):
                    last = pe.matmul(bank[4 + p_][:, 0:T], wa2[:, p_ * P:(p_ + 1) * P], glr[:, :], start=True, stop=True)
                last.then_inc(sm["loga_pre"], 1)
                pe.wait_ge(sm["out_placed_act"], 2)
                pe.wait_ge(sm["out_placed_dve"], 2)
                turn = 0
                for n_ in range(8):
                    if n_:
                        pe.wait_ge(sm["qk_ready"], n_)
                    for n in level_tiles(n_):
                        rows = P if n < 2 else TS
                        if turn == 2:
                            pe.wait_ge(sm["loga_x"], 2)
                        if turn >= 3:
                            pe.wait_ge(sm["att_done"], 2 * turn - 4)
                        for h in range(H):
                            r, p_ = head(h)
                            q_ = gq if n_ == 0 else qt[:, n_ % 2]
                            k_ = gk if n_ == 0 else kt[:, n_ % 2]
                            last = pe.matmul(bank[2 * (turn % 3) + h % 2][0:rows, p_ * P:p_ * P + rows],
                                             k_[r, p_, n * P:n * P + rows], q_[r, p_, n * P:n * P + rows],
                                             start=True, stop=True)
                        last.then_inc(sm["qk_used"], 1)
                        turn += 1
                pe.wait_ge(sm["khat_ready"], 2)
                for n in range(NT):
                    rows = P if n < 2 else TS
                    for p_ in range(2):
                        last = pe.transpose(bank[6 + n // 2][0:rows, (n % 2) * 256 + p_ * P:(n % 2) * 256 + (p_ + 1) * P],
                                            kt[:, 0, p_, n * P:n * P + rows], cst_("ident"))
                last.then_inc(sm["knat_turned"], 1)
                pe.wait_ge(sm["knat_ready"], 2)
                pe.wait_ge(sm["att_done"], 2 * turn)
                for ch in range(2):
                    for h in range(H):
                        r, p_ = head(h)
                        last = pe.matmul(bank[4 + ch][r, p_ * DV:(p_ + 1) * DV],
                                         kn[:, ch, h * DK:(h + 1) * DK], gv[:, ch, h * DV:(h + 1) * DV], start=True, stop=True)
                    last.then_inc(sm["s1_prod"], 1)
                pe.wait_ge(sm["knm_ready"], 1)
                pe.wait_ge(sm["att_done"], 2 * turn)
                for b in range(DB):
                    for h in range(H):
                        r, p_ = head(h)
                        c0 = (b % 2) * 256 + p_ * DV
                        last = pe.matmul(bank[b // 2][r, c0:c0 + DV], knm[:, b, h * DK:(h + 1) * DK],
                                         gv[0:TS, 2, h * DV:(h + 1) * DV], start=True, stop=True)
                last.then_inc(sm["st_prod"], 1)
                for h in range(H):
                    r, p_ = head(h)
                    out = bank[O_BANK[h]]
                    if h == 0:
                        pe.wait_ge(sm["s1_ready"], 1)
                    if h == 2:
                        pe.wait_ge(sm["s2_ready"], 2)
                    vh = slice(h * DV, (h + 1) * DV)

                    def mm(o, lhs, rhs, first=False, end=False):
                        return pe.matmul(o, lhs, rhs, start=first, stop=end, skip_group_check=True)
                    mm(out[:, 0:P], gv[:, 0, vh], att[:, 0, h, :], True)
                    mm(out[:, P:TP], gv[:, 1, vh], att[:, 1, h, :])
                    mm(out[:, TP:T], gv[:, 2, vh], att[:, 2, h, 0:TS])
                    mm(out[:, P:TP], s1[r, p_, :], qt[r, 0, p_, P:TP])
                    for b in range(DB):
                        c0 = TP + DT * b
                        last = mm(out[:, c0:c0 + DT], st[r, b, p_, :], qt[r, 0, p_, c0:c0 + DT], end=(b == DB - 1))
                    last.then_inc(sm["o_prod"], 1)
                pe.wait_ge(sm["st_done"], 16)
                for h in range(H):
                    pe.wait_ge(sm["o_sq"], h + 1)
                    pe.matmul(bank[h][:, 0:T], cst_("mean_dv"), osq[:, h, :], start=True, stop=True).then_inc(sm["o_mean"], 1)

                pe.wait_ge(sm["conv_y"], 1)
                pe.wait_ge(sm["o_done"], 4)
                for c in range(2):
                    last = pe.matmul(bank[4][:, 0:T], cst_("mean_ch"), yT[:, c, :], start=(c == 0), stop=(c == 1))
                last.then_inc(sm["conv_mean"], 1)
                pe.wait_ge(sm["conv_v"], 2)
                for c in range(2):
                    last = pe.matmul(bank[5][:, 0:T], cst_("mean_ch"), sq[:, c, :], start=(c == 0), stop=(c == 1))
                last.then_inc(sm["conv_var"], 1)

                pe.wait_ge(sm["qb_ready"], 4)
                for g in range(DB // G):
                    for p_ in range(2):
                        for b in range(G):
                            c0 = (G * g + b) * 32
                            last = pe.matmul(bank[0][32 * b:32 * b + 32, TP + g * TS:TP + (g + 1) * TS], qb[:, p_, c0:c0 + 32],
                                             ks[:, p_, TP:T], start=(p_ == 0), stop=(p_ == 1), skip_group_check=True)
                last.then_inc(sm["zn_prod"], 1)
                for h in range(H):
                    r, p_ = head(h)
                    pe.matmul(bank[2 * (h % 2)][:, p_ * P:(p_ + 1) * P], ks[r, p_, P:TP], qs[r, p_, P:TP], start=True, stop=True)
                    last = pe.matmul(bank[2 * (h % 2) + 1][:, p_ * TP:(p_ + 1) * TP], ks[r, p_, 0:P], qs[r, p_, 0:TP], start=True, stop=True)
                last.then_inc(sm["pz_prod"], 1)
                pe.wait_ge(sm["pz_sp"], 1)
                pe.wait_ge(sm["conv_r"], 1)
                for n in range(3):
                    pe.matmul(bank[4 + n][:, :], cst_("from_here"), ps_s[:, n, :], start=True, stop=(n == 0), skip_group_check=True)
                for p_ in range(2):
                    o = bank[5 + p_][:, :].rearrange("p (h t) -> p h t", h=2)[:, :, P:TP]
                    later = ps_s[:, 0, 2 * P * p_:2 * P * (p_ + 1)].rearrange("p (h t) -> p h t", h=2)
                    last = pe.matmul(o, cst_("ones"), later, start=False, stop=True, skip_group_check=True)
                last.then_inc(sm["pz_cum"], 1)
                pe.wait_ge(sm["pz_w"], 1)
                for h in range(H):
                    r, p_ = head(h)
                    c0 = p_ * TP
                    pe.matmul(bank[7][r, c0:c0 + TP], svn[:, 0, h * DK:(h + 1) * DK],
                              ps_z[:, 1 + p_, (h % 2) * TP:(h % 2 + 1) * TP], start=True, stop=False, skip_group_check=True)
                    last = pe.matmul(bank[7][r, c0 + P:c0 + TP], svn[:, 1, h * DK:(h + 1) * DK],
                                     ps_z[:, 0, h * P:(h + 1) * P], start=False, stop=True, skip_group_check=True)
                last.then_inc(sm["po_prod"], 1)
                pe.wait_ge(sm["wn_ready"], 1)
                for g in range(DB // G):
                    last = pe.transpose(bank[3][0:TS, g * P:(g + 1) * P], zn[:, g, :], cst_("ident"))
                last.then_inc(sm["wn_turned"], 1)
                pe.wait_ge(sm["po_done"], 1)
                pe.wait_ge(sm["wn_placed"], 1)

                def turn_keys(st_i):
                    pe.wait_ge(k_loaded[st_i % 2], P * (st_i // 2 + 1))
                    for b in range(G):
                        if st_i:
                            pe.wait_ge(sm[KT_SEM[b % 2]], 2 * st_i - 1 + b // 2)
                        for p_ in range(2):
                            for j in range(2):
                                last = pe.transpose(bank[b][:, p_ * 256 + j * P:p_ * 256 + (j + 1) * P],
                                                    kpg[:, st_i % 2, b, j, p_ * P:(p_ + 1) * P], cst_("ident"))
                        last.then_inc(sm["kt_turned"], 1)

                def scores(st_i):
                    it = st_i // 2
                    for k_ in KT_SEM:
                        pe.wait_ge(sm[k_], 2 * st_i + 2)
                    if st_i % 2 == 0 and it >= 2:
                        pe.wait_ge(sm["z_placed"], it - 1)
                    for p_ in range(2):
                        for b in range(G):
                            c0 = (it // (PAGES // 4) * G + b) * 32
                            last = pe.matmul(bank[4 + it % 2][32 * b:32 * b + 32, st_i % 2 * 256:(st_i % 2 + 1) * 256],
                                             qb[:, p_, c0:c0 + 32], kT[:, st_i % 2, b, p_, :],
                                             start=(p_ == 0), stop=(p_ == 1), skip_group_check=True)
                    last.then_inc(sm["kt_used"], 1)

                def keys(it):
                    turn_keys(2 * it)
                    if it:
                        scores(2 * it - 1)
                    turn_keys(2 * it + 1)
                    scores(2 * it)

                def new_values(g):
                    if g:
                        pe.wait_ge(sm["so_done"], 4 * g)
                    pe.matmul(bank[7][:, 0:256], wTn[:, g, :], svn[:, 2, :], start=True, stop=False, skip_group_check=True)

                def values(it):
                    pe.wait_ge(sm["w_ready"], it + 1)
                    if it:
                        pe.wait_ge(sm["wt_placed"], it)
                    for j in range(4):
                        last = pe.transpose(bank[6][:, j * P:(j + 1) * P], w_[:, it % 2, j * P:(j + 1) * P], cst_("ident"))
                    last.then_inc(sm["wt_turned"], 1)
                    pe.wait_ge(sm["wt_placed"], it + 1)
                    pe.wait_ge(v_loaded[it % 2], 256 * (it // 2 + 1))
                    for j in range(4):
                        for b in range(G):
                            last = pe.matmul(bank[7][32 * b:32 * b + 32, 0:256], wT[:, it % 2, j, 32 * b:32 * b + 32],
                                             vpg[:, it % 2, b, j, :], start=False, stop=(j == 3 and it % 4 == 3), skip_group_check=True)
                    last.then_inc(sm["v_used"], 1)

                def outputs(g):
                    pe.wait_ge(sm["oq_placed"], g + 1)
                    for p_ in range(2):
                        last = pe.transpose(bank[7][:, 256 + p_ * P:256 + (p_ + 1) * P], oq[:, p_ * P:(p_ + 1) * P], cst_("ident"))
                    last.then_inc(sm["oq_turned"], 1)

                new_values(0)
                for it in range(ITS):
                    keys(it)
                    if it == ITS - 1:
                        scores(2 * it + 1)
                    if it:
                        values(it - 1)
                    if it == 4:
                        outputs(0)
                        new_values(1)
                values(ITS - 1)
                outputs(1)

                pe.wait_ge(sm["so_done"], 8)
                for n in range(KD):
                    if n >= 2:
                        pe.wait_ge(sm["f_ready"], 8 + n - 1)
                    unit(U_OUT + n, bank[4 + n % 2][:, 0:T], hh, hl, KD, first_wait=sm["mix_lo"] if n == 0 else None)
                post_norm(1)
                ffn(1, U_FFN2)

            @block.scalar
            def _(act):
                A = Steps(act, sm["act_step"])
                nsa = nc.scalar.activation

                def hi(u, n=8):
                    if isinstance(u, int):
                        if u >= U_END:
                            return
                        slot = u % SLOTS
                        if u >= SLOTS:
                            act.wait_ge(sm["w_used"], u - SLOTS + 1)
                        act.wait_ge(w_loaded[slot], 16 * (u // SLOTS + 1))
                    else:
                        c, v = u
                        slot = c % SLOTS
                        act.wait_ge(sm["w_used"], v + (c - SLOTS + 1))
                        act.wait_ge(w_loaded[slot], v * (16 // SLOTS) + 16 * (c // SLOTS + 1))
                    A(nsa(w_h[:, slot, 0:n, :], raw[:, slot, 0:n, :], ACT.Copy), sm["w_hi"])

                def rsqrt(mean, out, tmp, done):
                    A(nsa(tmp, mean, ACT.Ln, bias=cst_("eps")))
                    A.settle()
                    return A(nsa(out, tmp, ACT.Exp, scale=-0.5), done)

                def exp_ln():
                    act.preload_act_table_set("natural_log_exp_and_others")

                def pre_norm(c):
                    exp_ln()
                    for j in range(KD):
                        if c:
                            act.wait_ge(sm["x_ready"], 8 * (c - 1) + j + 1)
                        if 8 * c + j >= 2:
                            act.wait_ge(sm["sq_used"], 8 * c + j - 1)
                        if j < 2:
                            act.wait_ge(sm["ss_done"], 8 * c) if c else None
                        A(nsa(sq[:, j % 2, :], xT[:, j, :], ACT.Square), sm["sq_ready"])
                    act.wait_ge(sm["sq_used"], 8 * c + 8)
                    rsqrt(bank[6][:, 0:T], rs[:, :], rln[:, :], sm["r_ready"])
                    for j in range(KD):
                        act.wait_ge(sm["h_ready"], 8 * c + j + 1)
                        A(nsa(hh[:, j, 0:T], ht[:, j % 2, :], ACT.Copy), sm["h_hi"])

                def evac_f(c, n, u, i=None, unguarded=False):
                    add = 0 if i is None else 4 * i
                    act.wait_ge(sm["w_used"], u)
                    A(nsa(fT[:, (n if i is None else bass.ds(i * 4 + n, 1)), :].rearrange("p a t -> p (a t)") if i is not None else fT[:, n, :],
                          bank[4 + n % 2][:, 0:T], ACT.Copy), sm["f_ready"])
                    A.settle()
                    if not unguarded:
                        act.wait_ge(sm["ss_done"], 8 * c + n - 1 + add)
                    src = fT[:, n, :] if i is None else fT[:, bass.ds(i * 4 + n, 1), :].rearrange("p a t -> p (a t)")
                    A(nsa(sq[:, n % 2, :], src, ACT.Square), sm["fsq_ready"])

                def post_norm(c):
                    exp_ln()
                    act.wait_ge(sm["post_mean"], c + 1)
                    rsqrt(bank[6][:, 0:T], rs[:, :], rln[:, :], sm["r_ready"])

                def ffn(k, U0):
                    c = 2 * k
                    pre_norm(c)

                    def pair(i, u, n, peeled):
                        for t in range(2):
                            c0, v = u(2 * t)
                            act.wait_ge(sm["w_used"], v + (c0 + 1))
                            if not (peeled and k == 0):
                                act.wait_ge(sm["gate_up"], (k * FT + t - 1 if not peeled else k * FT) + (0 if peeled else 2 * i))
                            A(nsa(sg[:, t, :], bank[2 * t][:, 0:T], ACT.Silu), sm["gate_act"])
                            for m in range(2):
                                x = u(2 * t + m + LEAD)
                                hi(x if not peeled else x[0] + x[1], n[2 * t + m])
                            act.wait_ge(sm["gate_up"], k * FT + t + 1 + 2 * i)
                            dst = guh[:, t, :] if peeled else guh[:, bass.ds(i * 2 + t, 1), :].rearrange("p a t -> p (a t)")
                            A(nsa(dst, gt[:, t, :], ACT.Copy), sm["gu_hi"])
                    pair(0, lambda j: (U0 + j, 0), [8] * 4, True)
                    per = [(sm["gate_act"], 2), (sm["gu_hi"], 2), (sm["w_hi"], 4)]
                    with A.repeat(1, FT // 2, per) as i:
                        pair(i, lambda j: (U0 + j, i * 4), [8] * 4, False)
                    Ud = U0 + 2 * FT

                    def four(i, last):
                        for n in range(4):
                            for m in range(3):
                                nxt = 12 * i + 3 * n + m + LEAD
                                hi(Ud + nxt, DOWN[nxt % 3][1] if nxt < 24 else 8)
                            evac_f(c, 4 * i + n, Ud + 12 * i + 3 * n + 3, unguarded=(4 * i + n < 2))
                    four(0, False)
                    four(1, k == 1)
                    post_norm(c)

                act.wait_ge(sm["par_turned"], 1)
                A(nsa(par[:, :], bank[7][:, 0:NPAR], ACT.Copy), sm["par_ready"])
                for u in range(LEAD):
                    hi(u)
                ffn(0, 0)
                pre_norm(1)

                act.wait_ge(sm["cst_turned"], 1)
                for g in range(2):
                    for c in range(2):
                        dst = ext[:, c, HALO + TP:].rearrange("p (b t) -> p b t", b=DB)[:, 4 * g:4 * g + 4, 0:HALO]
                        A(nsa(dst, bank[7][:, (2 * g + c) * 120:(2 * g + c + 1) * 120].rearrange("p (b t) -> p b t", b=4), ACT.Copy), sm["cst_placed"])
                for m, (what, c, _) in enumerate(UNITS_IN):
                    b_ = bank[m % 4][:, 0:T]
                    if what in ON_ACT:
                        act.wait_ge(sm["w_used"], U_IN + m + 1)
                        if what == "g":
                            A(nsa(sq[:, c, :], b_, ACT.Sigmoid), sm["zin_act"])
                        elif what == "gg":
                            A(nsa(gate[:, c, :], b_, ACT.Silu), sm["zin_act"])
                        elif what == "glr":
                            A(nsa(glr[:, :], bank[m % 4][0:16, 0:T], ACT.Copy), sm["zin_act"])
                        elif what == "sk":
                            A(nsa(ks[:, c, :], b_, ACT.Copy), sm["zin_act"])
                        else:
                            A(nsa((gq if what == "gq" else qs)[:, c, :], b_, ACT.Copy, scale=DK ** -0.5), sm["zin_act"])
                    hi(U_IN + m + LEAD)
                act.wait_ge(sm["par_ready"], 1)
                act.wait_ge(sm["qb_clear"], 1)
                A.settle()
                for h2 in range(2):
                    r = slice(h2 * DK, (h2 + 1) * DK)
                    for p_ in range(2):
                        dst = qb[r, p_, :].rearrange("p (b h q) -> p b h q", h=H, q=DT)[:, :, 2 * p_ + h2, :]
                        A(nsa(dst, qs[r, p_, TP:T].rearrange("p (b q) -> p b q", q=DT), ACT.Copy), sm["qb_ready"])
                act.wait_ge(sm["out_turned"], 2)
                A(nsa(skn[:, 0:2, :], bank[0][:, :].rearrange("p (n c) -> p n c", n=2), ACT.Copy), sm["out_placed_act"])
                A(nsa(skn[0:TS, 2, :], bank[1][0:TS, 0:256], ACT.Copy), sm["out_placed_act"])

                exp_ln()
                act.wait_ge(sm["loga_pre"], 1)
                for p_ in range(2):
                    A(nsa(dd[:, 0, p_, :], bank[4 + p_][:, 0:T], ACT.Identity, bias=par[:, PAR["gla_b_a"] + p_:PAR["gla_b_a"] + p_ + 1]), sm["loga_x"])
                act.wait_ge(sm["loga_neg"], 1)
                A(nsa(dd[:, 1], dd[:, 1], ACT.Exp))
                A.settle()
                A(nsa(dd[:, 1], dd[:, 1], ACT.Ln, bias=1.0), sm["loga_l"])
                for n_ in range(1, 8):
                    act.wait_ge(sm["qk_d"], n_)
                    d = dd[:, n_ % 2, :, 0:T if n_ <= 3 else TP]
                    A(nsa(d, d, ACT.Abs))
                    A.settle()
                    A(nsa(d, d, ACT.Exp, scale=-1.0 / 16), sm["qk_e"])
                act.wait_ge(sm["khat_d"], 2)
                A(nsa(dd[:, 0], dd[:, 0], ACT.Exp, scale=1.0 / 16), sm["khat_e"])
                A(nsa(dd[:, 1], bb[:, :, :], ACT.Exp, scale=1.0 / 16), sm["khat_e"])
                A(nsa(aend[:, :, 0:2], bb[:, :, P - 1:TP:P], ACT.Exp, scale=1.0 / 16), sm["khat_e"])
                A(nsa(aend[:, :, 2:10], bb[:, :, TP + DT - 1:T:DT], ACT.Exp, scale=1.0 / 16), sm["khat_e"])
                act.wait_ge(sm["knat_turned"], 1)
                A(nsa(kn[:, 0:2, :], bank[6][:, :].rearrange("p (n c) -> p n c", n=2), ACT.Copy), sm["knat_ready"])
                A(nsa(kn[0:TS, 2, :], bank[7][0:TS, 0:256], ACT.Copy), sm["knat_ready"])
                act.wait_ge(sm["s1_prod"], 1)
                A(nsa(s1[:, :, :].rearrange("p a v -> p (a v)"), bank[4][:, 0:256], ACT.Copy), sm["s1_ready"])
                for h in range(H):
                    act.wait_ge(sm["o_prod"], h + 1)
                    A(nsa(osq[:, h, :], bank[O_BANK[h]][:, 0:T], ACT.Square), sm["o_sq"])
                for h in range(H):
                    act.wait_ge(sm["o_mean"], h + 1)
                    rsqrt(bank[h][:, 0:T], osq[:, h, :], rln[:, :], sm["o_r"])
                    A.settle()

                for c in range(2):
                    act.wait_ge(sm["conv_d"], c + 1)
                    A(nsa(sq[:, c, :], yT[:, c, :], ACT.Square), sm["conv_v"])
                act.wait_ge(sm["conv_var"], 1)
                rsqrt(bank[5][:, 0:T], rs[:, :], rln[:, :], sm["conv_r"])

                act.wait_ge(sm["pz_neg"], 1)
                A(nsa(ps_t[:, :, :], ps_t[:, :, :], ACT.Exp))
                A.settle()
                A(nsa(ps_t[:, :, :], ps_t[:, :, :], ACT.Ln, bias=1.0), sm["pz_l"])
                act.wait_ge(sm["zn_neg"], 1)
                A(nsa(tn[:, :, :], tn[:, :, :], ACT.Exp))
                A.settle()
                A(nsa(tn[:, :, :], tn[:, :, :], ACT.Ln, bias=1.0), sm["zn_l"])
                act.wait_ge(sm["pz_lw"], 3)
                A(nsa(ps_z[:, :, :], ps_z[:, :, :], ACT.Exp), sm["pz_w"])
                act.wait_ge(sm["zn_lw"], 1)
                A(nsa(zn[:, :, :], zn[:, :, :], ACT.Exp), sm["wn_ready"])
                act.wait_ge(sm["wn_turned"], 1)
                A(nsa(wTn[0:TS, :, :].rearrange("p g c -> p (g c)"), bank[3][0:TS, 0:256], ACT.Copy), sm["wn_placed"])
                act.wait_ge(sm["po_prod"], 1)
                A(nsa(fT[:, 4:6, 0:TP], bank[7][:, :].rearrange("p (a t) -> p a t", a=2), ACT.Copy), sm["po_done"])
                act.wait_ge(sm["conv_n"], 2)
                for c in range(2):
                    A(nsa(fT[:, 6 + c, :], yT[:, c, :], ACT.Silu, bias=par[:, PAR["conv_norm_b"] + c:PAR["conv_norm_b"] + c + 1]), sm["conv_done"])
                exp_ln()

                def keys(it):
                    for st_i in (2 * it, 2 * it + 1):
                        for b in (0, 2):
                            act.wait_ge(sm["kt_turned"], 4 * st_i + b + 1)
                            if st_i >= 2:
                                act.wait_ge(sm["kt_used"], st_i - 1)
                            A(nsa(kT[:, st_i % 2, b].rearrange("p a c -> p (a c)"), bank[b][:, :], ACT.Copy), sm["kt_act"])

                def softplus(it):
                    t = t_[:, it % 2, :]
                    act.wait_ge(sm["z_placed"], it + 1)
                    if it >= 2:
                        act.wait_ge(sm["lw_ready"], it - 1)
                    A(nsa(t, z_[:, it % 2, :], ACT.Abs))
                    A.settle()
                    A(nsa(t, t, ACT.Exp, scale=-1.0))
                    A.settle()
                    A(nsa(t, t, ACT.Ln, bias=1.0), sm["z_l"])

                def weights(it):
                    act.wait_ge(sm["lw_ready"], it + 1)
                    if it >= 2:
                        act.wait_ge(sm["wt_turned"], it - 1)
                    A(nsa(w_[:, it % 2, :], z_[:, it % 2, :], ACT.Exp), sm["w_ready"])

                for it in range(ITS):
                    keys(it)
                    if it:
                        weights(it - 1)
                    softplus(it)
                weights(ITS - 1)

                act.wait_ge(sm["so_done"], 8)
                act.wait_ge(sm["o_done"], 4)
                A.settle()
                for j in range(KD):
                    A(nsa(hh[:, j, 0:T], fT[:, j, :], ACT.Copy), sm["mix_hi"])
                act.wait_ge(sm["mix_lo"], KD)
                for n in range(KD):
                    hi(U_OUT + n + LEAD)
                    evac_f(1, n, U_OUT + n + 1, unguarded=(n < 2))
                post_norm(1)
                ffn(1, U_FFN2)

            @block.vector
            def _(dve):
                V = Steps(dve, sm["dve_step"])

                def lo(u, n=8):
                    if isinstance(u, int):
                        if u >= U_END:
                            return
                        slot = u % SLOTS
                        dve.wait_ge(sm["w_hi"], u + 1)
                    else:
                        c, v = u
                        slot = c % SLOTS
                        dve.wait_ge(sm["w_hi"], v + (c + 1))
                    V(dve.tensor_tensor(w_l[:, slot, 0:n, :], raw[:, slot, 0:n, :], w_h[:, slot, 0:n, :].bitcast(F32), ALU.subtract), sm["w_lo"])

                def pre_norm(c):
                    g0 = 8 * c
                    dve.wait_ge(sm["r_ready"], 2 * c + 1)

                    def mul(j):
                        if 8 * c + j >= 2:
                            dve.wait_ge(sm["h_lo"], 8 * c + j - 1)
                        V(dve.scalar_tensor_tensor(ht[:, j % 2, :], xT[:, j, :], par[:, g0 + j:g0 + j + 1], rs[:, :], ALU.mult, ALU.mult), sm["h_ready"])
                    mul(0)
                    for j in range(KD):
                        if j + 1 < KD:
                            mul(j + 1)
                        dve.wait_ge(sm["h_hi"], 8 * c + j + 1)
                        V(dve.tensor_tensor(hl[:, j, 0:T], ht[:, j % 2, :], hh[:, j, 0:T].bitcast(F32), ALU.subtract), sm["h_lo"])

                def add_square(c, n):
                    dve.wait_ge(sm["fsq_ready"], 8 * c + n + 1)
                    V.settle()
                    V(dve.tensor_tensor(ss[:, :], ss[:, :], sq[:, n % 2, :], ALU.add), sm["ss_done"])

                def post_norm(c):
                    g0 = 24 + 8 * c
                    dve.wait_ge(sm["r_ready"], 2 * c + 2)

                    def term(j):
                        if j >= 2:
                            dve.wait_ge(sm["x_ready"], 8 * c + j - 1)
                        V(dve.scalar_tensor_tensor(ht[:, j % 2, :], fT[:, j, :], par[:, g0 + j:g0 + j + 1], rs[:, :], ALU.mult, ALU.mult), sm["dve_step"])
                        return V.last
                    done = term(0)
                    for j in range(KD):
                        nxt = term(j + 1) if j + 1 < KD else None
                        dve.wait_ge(*done)
                        V(dve.tensor_tensor(xT[:, j, :], xT[:, j, :], ht[:, j % 2, :], ALU.add), sm["x_ready"])
                        done = nxt

                def ffn(k, U0):
                    c = 2 * k
                    pre_norm(c)
                    V(dve.memset(ss[:, :], 0.0))

                    def pair(i, u, peeled):
                        for t in range(2):
                            x = [u(2 * t + m + LEAD) for m in range(2)]
                            x = [a_ + b_ for a_, b_ in x] if peeled else x
                            lo(x[0])
                            c0, v = u(2 * t + 1)
                            dve.wait_ge(sm["w_used"], v + (c0 + 1))
                            dve.wait_ge(sm["gate_act"], k * FT + t + 1 + 2 * i)
                            if not (peeled and k == 0):
                                dve.wait_ge(sm["gu_lo"], k * FT if peeled else k * FT + t - 1 + 2 * i)
                            V(dve.tensor_tensor(gt[:, t, :], sg[:, t, :], bank[2 * t + 1][:, 0:T], ALU.mult), sm["gate_up"])
                            lo(x[1])
                            dve.wait_ge(sm["gu_hi"], k * FT + t + 1 + 2 * i)
                            if peeled:
                                d, h_ = gul[:, t, :], guh[:, t, :]
                            else:
                                f = bass.ds(i * 2 + t, 1)
                                d, h_ = (g[:, f, :].rearrange("p a t -> p (a t)") for g in (gul, guh))
                            V(dve.tensor_tensor(d, gt[:, t, :], h_.bitcast(F32), ALU.subtract), sm["gu_lo"])
                    pair(0, lambda j: (U0 + j, 0), True)
                    with V.repeat(1, FT // 2, [(sm["gate_up"], 2), (sm["gu_lo"], 2), (sm["w_lo"], 4)]) as i:
                        pair(i, lambda j: (U0 + j, i * 4), False)
                    Ud = U0 + 2 * FT
                    for i in range(2):
                        for n in range(4):
                            for m in range(3):
                                nxt = 12 * i + 3 * n + m + LEAD
                                lo(Ud + nxt, DOWN[nxt % 3][1] if nxt < 24 else 8)
                            add_square(c, 4 * i + n)
                    post_norm(c)

                V(dve.memset(qb[:, :, :], 0.0)) if False else None
                dve.wait_ge(sm["par_ready"], 1)
                for c in (24, 40):
                    V(dve.tensor_scalar(par[:, c:c + 8], par[:, c:c + 8], 0.5, None, ALU.mult), sm["half_ready"])
                for u in range(LEAD):
                    lo(u)
                V.settle()
                ffn(0, 0)
                pre_norm(1)

                dve.wait_ge(sm["w_used"], U_IN)
                V(dve.memset(qb[:, :, :], 0.0), sm["qb_clear"])
                for c in range(2):
                    V(dve.memset(ext[:, c, 0:HALO], 0.0))
                V(dve.memset(wTn[:, :, :], 0.0))
                V(dve.memset(att[:, :, :, :], 0.0))
                V(dve.memset(qt[:, :, :, :], 0.0))
                V(dve.memset(kt[:, :, :, :], 0.0))

                def conv(k):
                    V.settle()
                    for c in range(2):
                        w = par[:, PAR["conv_w"] + 2 * k + c:PAR["conv_w"] + 2 * k + c + 1]
                        bias = par[:, PAR["conv_b"] + c:PAR["conv_b"] + c + 1]
                        v = ext[:, c, HALO + TP:].rearrange("p (b t) -> p b t", b=DB)[:, :, k:k + DT]
                        for out, x in ((yT[:, c, 0:TP], ext[:, c, k:k + TP]),
                                       (yT[:, c, TP:T].rearrange("p (b t) -> p b t", b=DB), v)):
                            if k == 0:
                                V(dve.tensor_scalar(out, x, w, bias, ALU.mult, ALU.add))
                            else:
                                V(dve.scalar_tensor_tensor(out, x, w, out, ALU.mult, ALU.add),
                                  sm["conv_y"] if k == TAPS - 1 and c == 1 and x is v else None)
                taps = 0
                g_seen = 0
                for m, (what, c, _) in enumerate(UNITS_IN):
                    lo(U_IN + m + LEAD)
                    if what == "g":
                        g_seen += 1
                        dve.wait_ge(sm["zin_act"], g_seen)
                        dve.wait_ge(sm["cst_placed"], 4)
                        a_ = bank[(m - 1) % 4]
                        V(dve.tensor_tensor(ext[:, c, HALO:HALO + TP], a_[:, 0:TP], sq[:, c, 0:TP], ALU.mult))
                        V(dve.tensor_tensor(ext[:, c, HALO + TP:].rearrange("p (b t) -> p b t", b=DB)[:, :, HALO:],
                                            a_[:, TP:T].rearrange("p (b t) -> p b t", b=DB),
                                            sq[:, c, TP:T].rearrange("p (b t) -> p b t", b=DB), ALU.mult), sm["zin_dve"])
                        V.settle()
                        V(dve.tensor_copy(cst[:, c, 0:DB * HALO].rearrange("p (b t) -> p b t", b=DB),
                                          ext[:, c, HALO + TP:].rearrange("p (b t) -> p b t", b=DB)[:, :, DT:]), sm["conv_packed"])
                    elif what in ("gk", "gv", "sv"):
                        dve.wait_ge(sm["w_used"], U_IN + m + 1)
                        if what == "gk":
                            V(dve.tensor_copy(gk[:, c, :], bank[m % 4][:, 0:T]), sm["zin_dve"])
                        else:
                            t = gv if what == "gv" else svn
                            V(dve.tensor_copy(t[:, :, c * P:(c + 1) * P], bank[m % 4][:, 0:NT * P].rearrange("p (n c) -> p n c", n=NT)), sm["zin_dve"])
                    if m >= 4:
                        for _ in range(2):
                            if taps < TAPS:
                                conv(taps)
                                taps += 1
                assert taps == TAPS
                dve.wait_ge(sm["out_turned"], 2)
                V(dve.tensor_copy(cso[0:4 * HALO, 0:2, :], bank[2][0:4 * HALO, :].rearrange("p (g c) -> p g c", g=2)), sm["out_placed_dve"])
                V(dve.tensor_copy(cso[0:HALO, 2, :], bank[3][0:HALO, 0:256]), sm["out_placed_dve"])

                dve.wait_ge(sm["loga_x"], 2)
                V(dve.scalar_tensor_tensor(dd[:, 1], dd[:, 0], -1.0, dd[:, 0], ALU.mult, ALU.min), sm["loga_neg"])
                dve.wait_ge(sm["loga_l"], 1)
                V(dve.scalar_tensor_tensor(dd[:, 0], dd[:, 0], 0.0, dd[:, 1], ALU.min, ALU.subtract))
                V.settle()
                for p_ in range(2):
                    V(dve.tensor_tensor_scan(bb[:, p_, :], cst_("gla_keep"), dd[:, 0, p_, :], 0.0, ALU.mult, ALU.add), sm["b_ready"])
                V.settle()

                def blocks(t, w, half=None):
                    if w <= 4:
                        v = t.rearrange("p a (n t) -> p (a n) t", t=2 * w)
                        return v if half is None else v[:, :, half * w:half * w + w]
                    v = t[:, :, 0:TP].rearrange("p a (n t) -> p a n t", t=2 * w)
                    return v if half is None else v[:, :, :, half * w:half * w + w]

                def decay(n_):
                    w = LEVELS[n_ - 1]
                    x = blocks(bb[:, :, :], w)
                    ref = x[:, :, w - 1:w] if w <= 4 else x[:, :, :, w - 1:w]
                    V.settle()
                    V(dve.tensor_tensor(blocks(dd[:, n_ % 2], w), x, ref.to_broadcast(x.shape), ALU.subtract), sm["qk_d"])

                used = [0]
                for n_ in range(8):
                    used.append(used[-1] + len(level_tiles(n_)))

                def scale(n_):
                    w = LEVELS[n_ - 1]
                    i = n_ % 2
                    dve.wait_ge(sm["qk_e"], n_)
                    if n_ >= 3:
                        dve.wait_ge(sm["qk_used"], used[n_ - 1])
                    V(dve.tensor_tensor(blocks(qt[:, i], w, 1), blocks(gq[:, :, :], w, 1), blocks(dd[:, i], w, 1), ALU.mult))
                    V(dve.tensor_tensor(blocks(kt[:, i], w, 0), blocks(gk[:, :, :], w, 0), blocks(dd[:, i], w, 0), ALU.mult), sm["qk_ready"])

                def place(n_):
                    for i, n in enumerate(level_tiles(n_)):
                        rows = P if n < 2 else TS
                        dve.wait_ge(sm["qk_used"], used[n_] + i + 1)
                        V.settle()
                        for h2 in range(2):
                            scores = bank[2 * ((used[n_] + i) % 3) + h2][0:rows, 0:2 * P].rearrange("p (h t) -> p h t", h=2)
                            V(dve.copy_predicated(att[0:rows, n, h2::2, 0:rows],
                                                  level[0:rows, n_:n_ + 1, 0:rows].to_broadcast([rows, 2, rows]),
                                                  scores[:, :, 0:rows]), sm["att_done"])
                decay(1)
                decay(2)
                for n_ in range(1, 8):
                    scale(n_)
                    if n_ + 2 < 8:
                        decay(n_ + 2)
                    place(n_ - 1)
                place(7)
                V.settle()
                for d, x in ((dd[:, 0, :, 0:TP], bb[:, :, 0:TP]), (dd[:, 0, :, TP:T], bb[:, :, TP:T])):
                    n = P if x.shape[2] == TP else DT
                    x = x.rearrange("p a (n t) -> p a n t", t=n)
                    V(dve.tensor_tensor(d.rearrange("p a (n t) -> p a n t", t=n), x[:, :, :, n - 1:n].to_broadcast(x.shape), x, ALU.subtract), sm["khat_d"])
                dve.wait_ge(sm["khat_e"], 4)
                V(dve.tensor_tensor(kt[:, 0], gk[:, :, :], dd[:, 0], ALU.mult), sm["khat_ready"])
                V(dve.tensor_tensor(qt[:, 0], gq[:, :, :], dd[:, 1], ALU.mult), sm["khat_ready"])
                dve.wait_ge(sm["knat_ready"], 2)
                V(dve.tensor_tensor(knm[:, :, :], kn[0:TS, 2:3, :].to_broadcast([TS, DB, 256]),
                                    cst_("batch_of", TS).unsqueeze(2).to_broadcast([TS, DB, 256]), ALU.mult), sm["knm_ready"])
                dve.wait_ge(sm["s1_ready"], 1)
                dve.wait_ge(sm["s1_prod"], 2)
                for p_ in range(2):
                    V(dve.scalar_tensor_tensor(s2[:, p_, :], s1[:, p_, :], aend[:, p_, 1:2], bank[5][:, p_ * DV:(p_ + 1) * DV], ALU.mult, ALU.add), sm["s2_ready"])
                dve.wait_ge(sm["o_prod"], 4)
                for b in range(DB):
                    for p_ in range(2):
                        c0 = (b % 2) * 256 + p_ * DV
                        V(dve.scalar_tensor_tensor(st[:, b, p_, :], st[:, b, p_, :], aend[:, p_, 2 + b:3 + b], bank[b // 2][:, c0:c0 + DV], ALU.mult, ALU.add), sm["st_done"])
                for h in range(H):
                    dve.wait_ge(sm["o_r"], h + 1)
                    V(dve.scalar_tensor_tensor(fT[:, h, :], bank[O_BANK[h]][:, 0:T], par[:, PAR["gla_norm"] + h:PAR["gla_norm"] + h + 1], osq[:, h, :], ALU.mult, ALU.mult))
                    V.settle()
                    V(dve.tensor_tensor(fT[:, h, :], fT[:, h, :], gate[:, h, :], ALU.mult), sm["o_done"])

                dve.wait_ge(sm["conv_mean"], 1)
                for c in range(2):
                    V(dve.tensor_tensor(yT[:, c, :], yT[:, c, :], bank[4][:, 0:T], ALU.subtract), sm["conv_d"])
                dve.wait_ge(sm["conv_r"], 1)
                for c in range(2):
                    g = PAR["conv_norm_g"] + c
                    V(dve.scalar_tensor_tensor(yT[:, c, :], yT[:, c, :], par[:, g:g + 1], rs[:, :], ALU.mult, ALU.mult), sm["conv_n"])

                dve.wait_ge(sm["pz_prod"], 1)
                dve.wait_ge(sm["state_out"], 16 * 10)
                for h in range(H):
                    bias = sbb[:, h:h + 1]
                    V(dve.scalar_tensor_tensor(ps_z[:, 0, h * P:(h + 1) * P], bank[2 * (h % 2)][:, h // 2 * P:(h // 2 + 1) * P], bias, cst_("causal"), ALU.add, ALU.add))
                    c0 = (h % 2) * TP
                    o, i = ps_z[:, 1 + h // 2, c0:c0 + TP], bank[2 * (h % 2) + 1][:, h // 2 * TP:(h // 2 + 1) * TP]
                    V(dve.scalar_tensor_tensor(o[:, 0:P], i[:, 0:P], bias, cst_("causal"), ALU.add, ALU.add))
                    V(dve.tensor_scalar(o[:, P:TP], i[:, P:TP], bias, None, ALU.add))
                V.settle()
                V(dve.scalar_tensor_tensor(ps_t[:, :, :], ps_z[:, :, :], -1.0, ps_z[:, :, :], ALU.mult, ALU.min), sm["pz_neg"])
                dve.wait_ge(sm["zn_prod"], 1)
                V(dve.tensor_tensor(tn[:, 0, 0:H], cst_("head_of"), sbb[:, :], ALU.mult))
                V.settle()
                V(dve.tensor_reduce(bq[:, :], tn[:, 0, 0:H], mybir.AxisListType.X, ALU.add))
                V.settle()
                V(dve.scalar_tensor_tensor(zn[:, :, :].rearrange("p g c -> p (g c)"), bank[0][:, TP:TP + 2 * TS], bq[:, :], cst_("new_mask"), ALU.add, ALU.add))
                V.settle()
                V(dve.scalar_tensor_tensor(tn[:, :, :], zn[:, :, :], -1.0, zn[:, :, :], ALU.mult, ALU.min), sm["zn_neg"])
                dve.wait_ge(sm["pz_l"], 1)
                V(dve.scalar_tensor_tensor(ps_s[:, :, :], ps_z[:, :, :], 0.0, ps_t[:, :, :], ALU.max, ALU.add), sm["pz_sp"])
                dve.wait_ge(sm["zn_l"], 1)
                V(dve.scalar_tensor_tensor(tn[:, :, :], zn[:, :, :], 0.0, tn[:, :, :], ALU.max, ALU.add))
                V.settle()
                for g in range(DB // G):
                    V(dve.tensor_tensor_scan(sn[:, g, ::-1], cst_("ones", cols=TS), tn[:, g, ::-1], 0.0, ALU.mult, ALU.add))
                V.settle()
                V(dve.tensor_tensor(zn[:, :, :], zn[:, :, :], sn[:, :, :], ALU.subtract), sm["zn_lw"])
                dve.wait_ge(sm["pz_cum"], 1)
                for n in range(3):
                    V(dve.tensor_tensor(ps_z[:, n, :], ps_z[:, n, :], bank[4 + n][:, :], ALU.subtract), sm["pz_lw"])

                dve.wait_ge(sm["pz_w"], 1)
                dve.wait_ge(sm["po_prod"], 1)

                def keys(it):
                    for st_i in (2 * it, 2 * it + 1):
                        for b in (1, 3):
                            dve.wait_ge(sm["kt_turned"], 4 * st_i + b + 1)
                            if st_i >= 2:
                                dve.wait_ge(sm["kt_used"], st_i - 1)
                            V(dve.tensor_copy(kT[:, st_i % 2, b].rearrange("p a c -> p (a c)"), bank[b][:, :]), sm["kt_dve"])

                def place_scores(it):
                    dve.wait_ge(sm["kt_used"], 2 * it + 2)
                    if it >= 2:
                        dve.wait_ge(sm["w_ready"], it - 1)
                    V(dve.tensor_scalar(z_[:, it % 2, :], bank[4 + it % 2][:, :], bq[:, :], None, ALU.add), sm["z_placed"])

                def log_weights(it):
                    z, t, s = z_[:, it % 2, :], t_[:, it % 2, :], s_[:, it % 2, :]
                    dve.wait_ge(sm["z_l"], it + 1)
                    V(dve.scalar_tensor_tensor(t, z, 0.0, t, ALU.max, ALU.add))
                    V.settle()
                    later = sn[:, it // 4, 0:1] if it % 4 == 0 else s_[:, 1 - it % 2, 0:1]
                    V(dve.tensor_tensor_scan(s[:, ::-1], cst_("ones", cols=1).to_broadcast([P, 512]), t[:, ::-1], later, ALU.mult, ALU.add))
                    V.settle()
                    V(dve.tensor_tensor(z, z, s, ALU.subtract), sm["lw_ready"])

                def weights(it):
                    dve.wait_ge(sm["wt_turned"], it + 1)
                    if it >= 2:
                        dve.wait_ge(sm["v_used"], it - 1)
                    V(dve.tensor_copy(wT[:, it % 2].rearrange("p n c -> p (n c)"), bank[6][:, :]), sm["wt_placed"])

                def outputs(g):
                    dve.wait_ge(sm["v_used"], 4 * g + 4)
                    if g:
                        dve.wait_ge(sm["oq_turned"], g)
                    V(dve.tensor_copy(oq[:, :], bank[7][:, 0:256]), sm["oq_placed"])
                    dve.wait_ge(sm["oq_turned"], g + 1)
                    for p_ in range(2):
                        for h2 in range(2):
                            r = slice(h2 * DK, (h2 + 1) * DK)
                            c0 = TP + 32 * g
                            src = bank[7][r, 256 + p_ * P:256 + (p_ + 1) * P].rearrange("p (b h q) -> p b h q", h=H, q=DT)[:, :, 2 * p_ + h2, :]
                            V(dve.tensor_copy(fT[r, 4 + p_, c0:c0 + 32].rearrange("p (b q) -> p b q", q=DT), src), sm["so_done"])

                for it in range(ITS):
                    keys(it)
                    if it:
                        weights(it - 1)
                    if it == 4:
                        outputs(0)
                    place_scores(it)
                    log_weights(it)
                weights(ITS - 1)
                outputs(1)
                V(dve.memset(hh[:, :, T:].bitcast(I32), 0))
                V(dve.memset(hl[:, :, T:].bitcast(I32), 0))

                dve.wait_ge(sm["conv_done"], 2)
                dve.wait_ge(sm["po_done"], 1)
                V.settle()
                for j in range(KD):
                    dve.wait_ge(sm["mix_hi"], j + 1)
                    V(dve.tensor_tensor(hl[:, j, 0:T], fT[:, j, :], hh[:, j, 0:T].bitcast(F32), ALU.subtract), sm["mix_lo"])
                V(dve.memset(ss[:, :], 0.0))
                for n in range(KD):
                    lo(U_OUT + n + LEAD)
                    add_square(1, n)
                post_norm(1)
                ffn(1, U_FFN2)

        clear()

    with nc.Block() as block:
        @block.tensor
        def _(pe):
            for n in range(NT):
                rows = P if n < 2 else TS
                for g in range(2):
                    for j in range(4):
                        last = pe.transpose(bank[2 * n + g][0:rows, j * P:(j + 1) * P], xT[:, 4 * g + j, n * P:n * P + rows], cst_("ident"))
                    last.then_inc(sm["y_turned"], 1)

        @block.vector
        def _(dve):
            for n in range(NT):
                rows = P if n < 2 else TS
                for g in range(2):
                    dve.wait_ge(sm["y_turned"], 2 * n + g + 1)
                    dve.tensor_copy(xn[0:rows, n, g * 512:(g + 1) * 512], bank[2 * n + g][0:rows, :]).then_inc(sm["y_placed"], 1)

        @block.sync
        def _(sp_):
            for n in range(2):
                sp_.wait_ge(sm["y_placed"], 2 * n + 2)
                sp_.dma_start(outs["y_prompt"][0, n * P:(n + 1) * P, :], xn[:, n, :]).then_inc(sm["x_stored"], 16)
            sp_.wait_ge(sm["y_placed"], 6)
            sp_.dma_start(outs["y_sample"].rearrange("b t d -> (b t) d"), xn[0:TS, 2, :]).then_inc(sm["x_stored"], 16)
            sp_.wait_ge(sm["x_stored"], 48)
    stack.close()


O_BANK = (6, 7, 4, 5)
KT_SEM = ("kt_act", "kt_dve")


def head(h):
    return slice((h % 2) * DK, (h % 2 + 1) * DK), h // 2


def level_tiles(n_):
    return range(NT if n_ <= 3 else 2)


ITS = DB // G * (PAGES // 4)


def first_page(it):
    return PAGES - 4 - it % (PAGES // 4) * 4


_INS = ["x_prompt", "x_sample", "cache_sb_k", "cache_sb_v", "page_table", "state_gla", "state_conv", "ffn1_norm_pre",
        "ffn1_norm_post", "ffn1_w_gate", "ffn1_w_up", "ffn1_w_down", "mix_norm_pre", "mix_norm_post", "w_in", "gla_w_a2",
        "gla_b_a", "gla_norm", "sb_bias", "conv_w", "conv_b", "conv_norm_g", "conv_norm_b", "w_out", "ffn2_norm_pre",
        "ffn2_norm_post", "ffn2_w_gate", "ffn2_w_up", "ffn2_w_down"]
_OUTS = [("y_prompt", (1, TP, D)), ("y_sample", (DB, DT, D)), ("prompt_sb_k", (L, 1, TP, H, DK)),
         ("prompt_sb_v", (L, 1, TP, H, DK)), ("prompt_gla_state", (L, 1, H, DK, DV)),
         ("prompt_conv_state", (L, 1, HALO, 256)), ("sample_sb_k", (L, DB, DT, H, DK)),
         ("sample_sb_v", (L, DB, DT, H, DK)), ("sample_gla_state", (L, DB, H, DK, DV)),
         ("sample_conv_state", (L, DB, HALO, 256))]


def kernel(**inputs):
    import concourse.bacc as bacc
    from concourse.bass_utils import run_bass_kernel_spmd

    nc = bacc.Bacc("TRN2", target_bir_lowering=False, num_devices=1)
    arrays = {f"in_{name}": np.ascontiguousarray(inputs[name]) for name in _INS}
    arrays["in_const"], arrays["in_level"] = CONST, LEVEL
    ins = {name[3:]: nc.dram_tensor(name, a.shape, mybir.dt.from_np(a.dtype), kind="ExternalInput").ap()
           for name, a in arrays.items()}
    outs = {name: nc.dram_tensor(f"out_{name}", shape, F32, kind="ExternalOutput").ap() for name, shape in _OUTS}
    build(nc, ins, outs)
    r = run_bass_kernel_spmd(nc, [arrays], core_ids=[0])
    return tuple(r.results[0][f"out_{name}"] for name, _ in _OUTS)
```

```python
from contextlib import ExitStack, contextmanager

import numpy as np

import concourse.bass as bass
from concourse import mybir

ALU = mybir.AluOpType
ACT = mybir.ActivationFunctionType
F32 = mybir.dt.float32
F32R = mybir.dt.float32r
U8 = mybir.dt.uint8
I32 = mybir.dt.int32

P = 128
D = 1024
F = 2816
KD = D // P
FT = F // P
L = 2
TP = 256
DB, DT = 8, 8
TS = DB * DT
T = TP + TS
NT = 3
G = 4
PAGES = 16
H = 4
DK = 64
DV = 128
TAPS = 31
HALO = TAPS - 1
EXT = HALO + TP + DB * (HALO + DT)
EPS = 1e-6
NEG = -1e30
SLOTS = 4
LEAD = 4
DOWN = ((0, 8), (8, 7), (15, 7))
LEVELS = (1, 2, 4, 8, 16, 32, 64)

UNITS_IN = ([("a", 0, 2320), ("g", 0, 2576), ("a", 1, 2448), ("g", 1, 2704)]
            + [("gg", c, 1024 + P * c) for c in range(4)] + [("glr", 0, 1536)]
            + [("gq", c, P * c) for c in range(2)] + [("gk", c, 256 + P * c) for c in range(2)]
            + [("sq", c, 1552 + P * c) for c in range(2)] + [("sk", c, 1808 + P * c) for c in range(2)]
            + [("gv", c, 512 + P * c) for c in range(4)]
            + [("sv", c, 2064 + P * c) for c in range(2)])
NIN = len(UNITS_IN)
EARLY_TAPS = 9
LEVEL0 = 13
U_FFN = 2 * FT + 3 * KD
U_IN = U_FFN
U_OUT = U_IN + NIN
U_FFN2 = U_OUT + KD
U_END = U_FFN2 + U_FFN

PAR = {}
_n = 0
for _name, _rows in (("ffn1_norm_pre", 8), ("mix_norm_pre", 8), ("ffn2_norm_pre", 8), ("ffn1_norm_post", 8),
                     ("mix_norm_post", 8), ("ffn2_norm_post", 8), ("gla_b_a", 2), ("gla_norm", 4), ("conv_b", 2),
                     ("conv_norm_g", 2), ("conv_norm_b", 2), ("conv_w", 2 * TAPS)):
    PAR[_name] = _n
    _n += _rows
NPAR = _n


def constants():
    i = np.arange(P)
    parts, at, n = [], {}, 0

    def put(name, a):
        nonlocal n
        full = np.zeros((P, a.shape[1]), np.float32)
        full[:a.shape[0]] = a
        at[name] = (n, n + a.shape[1])
        n += a.shape[1]
        parts.append(full)

    put("ident", np.eye(P))
    put("mean_d", np.full((P, P), 1.0 / D))
    put("mean_dv", np.full((P, P), 1.0 / DV))
    put("mean_ch", np.full((P, P), 1.0 / 256))
    put("ones", np.ones((P, P)))
    put("from_here", (i[:, None] >= i[None, :]).astype(np.float32))
    seg = np.ones(T)
    seg[[0, P]] = 0
    seg[TP::DT] = 0
    put("gla_keep", np.tile(seg, (P, 1)))
    put("causal", np.where(i[:, None] < i[None, :], 0, NEG))
    b, t = i[:TS] // DT, i[:TS] % DT
    qbatch, qhead, qt_ = i // 32, i // DT % H, i % DT
    mask = [np.where((b[None, :] == G * g + qbatch[:, None]) & (t[None, :] < qt_[:, None]), 0, NEG) for g in range(DB // G)]
    put("new_mask", np.concatenate(mask, 1))
    put("head_of", (qhead[:, None] == np.arange(H)[None, :]).astype(np.float32))
    put("batch_of", (b[:, None] == np.arange(DB)[None, :]).astype(np.float32))
    put("eps", np.full((P, 1), EPS))
    level = np.zeros((P, 8, P), np.int32)
    level[:, 0] = np.eye(P)
    for n_, w in enumerate(LEVELS):
        s, q = i[:, None], i[None, :]
        level[:, n_ + 1] = (s // (2 * w) == q // (2 * w)) & (s % (2 * w) < w) & (q % (2 * w) >= w)
    return np.concatenate(parts, 1), at, level.reshape(P, 8 * P)


CONST, AT, LEVEL = constants()


SEMAPHORES = """
const_loaded x_loaded x_stored x_turned x_placed par_loaded row_loaded state_loaded state_out
w_loaded0 w_loaded1 w_loaded2 w_loaded3 w_hi w_lo w_used act_step dve_step par_turned par_placed par_ready
sq_ready sq_used sx_done x_mean gate_r gt_ready r_ready h_ready h_hi h_lo v_turned v_placed x_ready gate_act gate_up gu_hi gu_lo f_ready fsq_ready ss_done post_mean
zin_act zin_dve qb_clear cst_turned cst_placed out_turned out_placed_act out_placed_dve
loga_pre loga_x loga_neg loga_l b_ready qk_d qk_e qk_ready qk_used att_done khat_d khat_e khat_ready
knat_turned knat_ready knm_ready s1_prod st_prod s1_ready s2_ready st_done o_prod o_sq o_mean o_r o_done
conv_packed conv_y conv_mean conv_d conv_v conv_var conv_r conv_n conv_done
qb_ready pz_prod pz_neg pz_l pz_sp pz_cum pz_lw pz_w po_done
zn_prod zn_neg zn_l zn_lw wn_ready
zn_s wn_turned wn_placed
k_loaded0 k_loaded1 v_loaded0 v_loaded1 kt_turned kt_act kt_dve kt_used z_placed z_l lw_ready w_ready wt_turned wt_placed v_used
po_prod oq_placed oq_turned so_done mix_hi mix_lo y_turned y_placed
"""


class Steps:

    def __init__(self, eng, own):
        self.eng, self.own, self.count, self.last = eng, own, {}, None
        self.per, self.turn = {}, 0

    def __call__(self, ins, sem=None):
        sem = self.own if sem is None else sem
        ins.then_inc(sem, 1)
        self.count[sem.name] = self.count.get(sem.name, 0) + 1
        self.last = (sem, self.count[sem.name])
        return ins

    def settle(self):
        sem, n = self.last
        per = self.per.get(sem.name, 0)
        self.eng.wait_ge(sem, self.turn * per + n if per else n)

    @contextmanager
    def repeat(self, start, stop, per):
        before = dict(self.count)
        self.per = {s.name: k for s, k in per}
        with self.eng.Fori(start, stop) as i:
            self.turn = i - start
            yield i
        for name, n in self.count.items():
            if n != before.get(name, 0):
                assert n - before.get(name, 0) == self.per.get(name), (name, n, before.get(name), self.per.get(name))
                self.count[name] = before.get(name, 0) + self.per[name] * (stop - start)
        self.last = (self.last[0], self.count[self.last[0].name])
        self.per, self.turn = {}, 0


def build(nc, ins, outs):
    stack = ExitStack()
    top = [nc.sbuf_base + 31 & ~31]

    def sb(name, shape, dt=F32, at=None):
        size = int(np.prod(shape[1:])) * (1 if dt == U8 else 4)
        size = size + 31 & ~31
        where = top[0] if at is None else at[0]
        if at is None:
            top[0] += size
        else:
            at[0] += size
        return nc.alloc_sbuf_tensor_at(name, shape, dt, offset=where)

    sems = []

    def sem(name):
        s = stack.enter_context(nc.semaphore(name))
        sems.append(s)
        return s

    const = sb("const", [P, CONST.shape[1]])
    level = sb("level", [P, 8, P], U8)
    xT = sb("xT", [P, KD, T])
    raw_at = top[0]
    raw = sb("raw", [P, SLOTS, 8, P])
    w_at = top[0]
    w_h = sb("w_h", [P, SLOTS, 8, P], F32R)
    w_l = sb("w_l", [P, SLOTS, 8, P], F32R)
    h_at = top[0]
    hh = sb("hh", [P, KD, T], F32R)
    hl = sb("hl", [P, KD, T], F32R)
    h_end = top[0]
    fT = sb("fT", [P, KD, T])
    sq = sb("sq", [P, 2, T])
    ss = sb("ss", [P, T])
    sx = sb("sx", [P, T])
    rs = sb("rs", [P, T])
    rln = sb("rln", [P, T])
    ht = sb("ht", [P, 2, T])
    par_all = sb("par_all", [P, L, NPAR])
    par = sb("par", [P, NPAR])
    sbb = sb("sbb", [P, H])
    wa2 = sb("wa2", [16, 256])
    pages = sb("pages", [1, DB * PAGES], I32)
    base = top[0]
    a = [base]
    guh = sb("guh", [P, FT, T], F32R, a)
    gul = sb("gul", [P, FT, T], F32R, a)
    sg = sb("sg", [P, 2, T], at=a)
    gt = sb("gt", [P, 2, T], at=a)
    gr = sb("gr", [P, 2, T], at=a)
    end_ffn = a[0]
    a = [base]
    qs = sb("qs", [P, 2, T], at=a)
    ks = sb("ks", [P, 2, T], at=a)
    svn = sb("svn", [P, NT, 256], at=a)
    yT = sb("yT", [P, 2, T], at=a)
    ext = sb("ext", [P, 2, EXT], at=a)
    qb = sb("qb", [P, 2, DB * 32], at=a)
    bq = sb("bq", [P, 1], at=a)
    zn = sb("zn", [P, DB // G, TS], at=a)
    tn = sb("tn", [P, DB // G, TS], at=a)
    sn = sb("sn", [P, DB // G, TS], at=a)
    wTn = sb("wTn", [P, DB // G, P], at=a)
    both = a[0]
    gate = sb("gate", [P, 4, T], at=a)
    gq = sb("gq", [P, 2, T], at=a)
    gk = sb("gk", [P, 2, T], at=a)
    gv = sb("gv", [P, NT, 512], at=a)
    glr = sb("glr", [16, T], at=a)
    bb = sb("bb", [P, 2, T], at=a)
    dd = sb("dd", [P, 2, 2, T], at=a)
    qt = sb("qt", [P, 2, 2, T], at=a)
    kt = sb("kt", [P, 2, 2, T], at=a)
    att = sb("att", [P, NT, H, P], at=a)
    att_end = a[0]
    st = sb("st", [P, DB, 2, DV], at=a)
    kn = sb("kn", [P, NT, 256], at=a)
    knm = sb("knm", [TS, DB, 256], at=a)
    aend = sb("aend", [P, 2, 10], at=a)
    s1 = sb("s1", [P, 2, DV], at=a)
    s2 = sb("s2", [P, 2, DV], at=a)
    osq = sb("osq", [P, H, T], at=a)
    end_gla = a[0]
    cst = sb("cst", [P, 2, 256], at=a)
    skn = sb("skn", [P, NT, 256], at=a)
    cso = sb("cso", [P, 3, 256], at=a)
    ps_z = sb("ps_z", [P, 3, 512], at=a)
    end_a = a[0]
    a = [both]
    kT = sb("kT", [P, 2, G, 2, 256], at=a)
    z_ = sb("z_", [P, 2, 512], at=a)
    t_ = sb("t_", [P, 2, 512], at=a)
    s_ = sb("s_", [P, 2, 512], at=a)
    w_ = sb("w_", [P, 2, 512], at=a)
    wT = sb("wT", [P, 2, 4, P], at=a)
    assert a[0] <= att_end
    oq = ht[:, 0, 0:256]
    a = [h_at]
    kpg = sb("kpg", [P, 2, G, 2, 256], at=a)
    assert a[0] <= h_end
    a = [raw_at]
    ps_t = sb("ps_t", [P, 3, 512], at=a)
    ps_s = sb("ps_s", [P, 3, 512], at=a)
    assert a[0] <= w_at
    a = [w_at]
    vpg = sb("vpg", [P, 2, G, 4, 256], at=a)
    assert a[0] <= h_at
    nc_end = max(end_ffn, end_a)
    assert nc_end <= nc.sbuf_usable_end, (nc_end, nc.sbuf_usable_end, end_ffn, end_a)
    xn = nc.alloc_sbuf_tensor_at("xn", [P, NT, D], F32, offset=base)
    parn = nc.alloc_sbuf_tensor_at("parn", [NPAR, L, P], F32, offset=base + NT * D * 4 + 8 * P * 4)
    level_in = nc.alloc_sbuf_tensor_at("level_in", [P, 8 * P], I32, offset=base + NT * D * 4)

    def in_bank(m):
        return bank[m % 4 if m < LEVEL0 else m % 2]

    def cst_(name, rows=P, cols=None):
        lo, hi = AT[name]
        return const[0:rows, lo:hi if cols is None else lo + cols]

    bank = [stack.enter_context(nc.psum_tensor(f"bank{i}", [P, 512], F32)) for i in range(8)]
    sm = {name: sem(name) for name in SEMAPHORES.split()}
    w_loaded = [sm[f"w_loaded{s}"] for s in range(SLOTS)]
    k_loaded = [sm["k_loaded0"], sm["k_loaded1"]]
    v_loaded = [sm["v_loaded0"], sm["v_loaded1"]]

    with nc.Block() as block:
        @block.sync
        def _(sp_):
            sp_.dma_start(const[:, :], ins["const"]).then_inc(sm["const_loaded"], 16)
            sp_.dma_start(level_in[:, :], ins["level"]).then_inc(sm["const_loaded"], 16)
            sp_.dma_start(pages[:, :], ins["page_table"].rearrange("(o b) n -> o (b n)", o=1)).then_inc(sm["const_loaded"], 16)
            sp_.dma_start(xn[:, 0:2, :], ins["x_prompt"].rearrange("o (n p) d -> p (o n) d", p=P)).then_inc(sm["x_loaded"], 16)
            sp_.dma_start(xn[0:TS, 2, :], ins["x_sample"].rearrange("b t d -> (b t) d")).then_inc(sm["x_loaded"], 16)

        @block.scalar
        def _(act):
            for name, at in PAR.items():
                src = ins[name].rearrange("l k (r c) -> (k r) l c", c=P) if name == "conv_w" else ins[name].rearrange("l (r c) -> r l c", c=P)
                act.dma_start(parn[at:at + src.shape[0], :, :], src).then_inc(sm["par_loaded"], 16)

        @block.tensor
        def _(pe):
            pe.wait_ge(sm["const_loaded"], 48)
            pe.wait_ge(sm["x_loaded"], 32)
            for j in range(KD):
                if j >= 4:
                    pe.wait_ge(sm["x_placed"], j - 3)
                for n in range(NT):
                    rows = P if n < 2 else TS
                    ins_ = pe.transpose(bank[j % 4][:, n * P:n * P + rows], xn[0:rows, n, j * P:(j + 1) * P],
                                        cst_("ident", rows, rows))
                ins_.then_inc(sm["x_turned"], 1)
            pe.wait_ge(sm["par_loaded"], 16 * len(PAR))
            for l in range(L):
                ins_ = pe.transpose(bank[4][:, l * P:l * P + NPAR], parn[:, l, :], cst_("ident", NPAR, NPAR))
            ins_.then_inc(sm["par_turned"], 1)

        @block.vector
        def _(dve):
            dve.wait_ge(sm["const_loaded"], 48)
            dve.tensor_copy(level[:, :, :].rearrange("p a b -> p (a b)"), level_in[:, :])
            for j in range(KD):
                dve.wait_ge(sm["x_turned"], j + 1)
                dve.tensor_copy(xT[:, j, :], bank[j % 4][:, 0:T]).then_inc(sm["x_placed"], 1)
            dve.wait_ge(sm["par_turned"], 1)
            dve.tensor_copy(par_all[:, :, :], bank[4][:, 0:L * P].rearrange("p (l c) -> p l c", l=L)[:, :, 0:NPAR]).then_inc(sm["par_placed"], 1)
            dve.wait_ge(sm["par_placed"], 1)
            for c in (24, 40):
                dve.tensor_scalar(par_all[:, :, c:c + 8], par_all[:, :, c:c + 8], 0.5, None, ALU.mult)
    def clear():
        nums = sorted(s.num for s in sems)
        assert nums == list(range(nums[0], nums[0] + len(nums)))
        nc.sync.sem_clear(range(nums[0], nums[-1] + 1))
        nc.all_engine_barrier()

    clear()

    with nc.Fori(0, L) as layer:
        one = bass.ds(layer, 1)

        def lay(ap, pattern, **kw):
            letters = pattern.split("->")
            return ap[one].rearrange("l " + letters[0] + "->" + letters[1].replace("*", "l"), **kw)

        def load_page(eng, dst, cache, it, b, n, loaded, free=None):
            at = (it // (PAGES // 4) * G + b) * PAGES + first_page(it) + n
            idx = eng.value_load(pages[0:1, at:at + 1], min_val=0, max_val=cache.shape[1] - 1)
            if free is not None:
                eng.wait_ge(*free)
            eng.dma_start(dst.rearrange("p (h d) -> p h d", h=H), cache[one, bass.ds(idx, 1)].rearrange("l n p h d -> p (l n h) d")).then_inc(loaded, 16)

        with nc.Block() as block:
            @block.sync
            def _(sp_):
                def load(u, src, n, static=True, first=False):
                    slot = (u if isinstance(u, int) else u[0]) % SLOTS
                    if isinstance(u, int):
                        if u >= SLOTS:
                            sp_.wait_ge(sm["w_lo"], u - SLOTS + 1)
                    else:
                        sp_.wait_ge(sm["w_lo"], u[1] + (u[0] - SLOTS + 1))
                    sp_.dma_start(raw[:, slot, 0:n, :], src).then_inc(w_loaded[slot], 16)

                def cols(w, k0, n, c):
                    src = w[one, k0 * P:(k0 + n) * P, c if isinstance(c, bass.DynSlice) else slice(c, c + P)]
                    return src.rearrange("l (k p) f -> p (l k) f", p=P)

                def ffn(U0, wg, wu, wd):
                    def pair(i, u):
                        for t in range(2):
                            c = bass.ds((2 * i + t) * P, P)
                            for m, w in ((0, wg), (1, wu)):
                                load(u(2 * t + m), cols(w, 0, KD, c), KD)
                    pair(0, lambda j: U0 + j)
                    with sp_.Fori(1, FT // 2) as i:
                        pair(i, lambda j: (U0 + j, i * 4))
                    Ud = U0 + 2 * FT

                    def four(i, u):
                        for n in range(4):
                            for m, (k0, kn_) in enumerate(DOWN):
                                load(u(3 * n + m), cols(wd, k0, kn_, bass.ds((4 * i + n) * P, P)), kn_)
                    with sp_.Fori(0, 2) as i:
                        four(i, lambda j: (Ud + j, i * 12))

                ffn(0, ins["ffn1_w_gate"], ins["ffn1_w_up"], ins["ffn1_w_down"])
                for m, (_, _, c) in enumerate(UNITS_IN):
                    load(U_IN + m, cols(ins["w_in"], 0, KD, c), KD)

                sp_.wait_ge(sm["w_used"], U_OUT)
                for it in range(ITS):
                    for s_i in range(2):
                        for b in range(G):
                            for j in range(2):
                                load_page(sp_, kpg[:, s_i, b, j, :], ins["cache_sb_k"], it, b, 2 * s_i + j, k_loaded[s_i],
                                          (sm["kt_turned"], 8 * it - 4 + 4 * s_i) if it and b == j == 0 else None)
                sp_.wait_ge(sm["pz_cum"], 1)
                for n in range(KD):
                    load(U_OUT + n, cols(ins["w_out"], 0, KD, n * P), KD)
                ffn(U_FFN2, ins["ffn2_w_gate"], ins["ffn2_w_up"], ins["ffn2_w_down"])

            @block.gpsimd
            def _(pool):
                pool.dma_start(wa2[:, :], ins["gla_w_a2"][one].rearrange("l r c -> (l r) c")).then_inc(sm["row_loaded"], 16)
                pool.dma_start(sbb[:, :], ins["sb_bias"][one].to_broadcast([P, H])).then_inc(sm["row_loaded"], 16)

                def sum_squares(k):
                    for j in range(KD):
                        pool.wait_ge(sm["sq_ready"], 16 * k + j + 1)
                        if j == 0:
                            if k:
                                pool.wait_ge(sm["x_mean"], k)
                            pool.tensor_copy(sx[:, :], sq[:, 0, :]).then_inc(sm["sx_done"], 1)
                        else:
                            pool.wait_ge(sm["sx_done"], 8 * k + j)
                            pool.tensor_tensor(sx[:, :], sx[:, :], sq[:, j % 2, :], ALU.add).then_inc(sm["sx_done"], 1)
                sum_squares(0)
                pool.wait_ge(sm["w_used"], U_IN)
                for p_ in range(2):
                    pool.dma_start(st[:, :, p_, :], ins["state_gla"][one, :, 2 * p_:2 * p_ + 2].rearrange("l b h k v -> (h k) (l b) v")).then_inc(sm["state_loaded"], 16)
                for g in range(2):
                    pool.dma_start(cst[0:4 * HALO, g, :], ins["state_conv"][one, 4 * g:4 * g + 4].rearrange("l b k c -> (l b k) c")).then_inc(sm["state_loaded"], 16)
                pool.wait_ge(sm["row_loaded"], 32)
                pool.wait_ge(sm["out_placed_act"], 2)
                pool.wait_ge(sm["out_placed_dve"], 2)
                pool.wait_ge(sm["v_placed"], 12)
                so = sm["state_out"]
                for name, t in (("k", skn), ("v", svn)):
                    pool.dma_start(outs["prompt_sb_" + name][one].rearrange("l o (n p) h d -> p (l o n) (h d)", p=P), t[:, 0:2, :]).then_inc(so, 16)
                    pool.dma_start(outs["sample_sb_" + name][one].rearrange("l b t h d -> (l b t) (h d)"), t[0:TS, 2, :]).then_inc(so, 16)
                pool.dma_start(outs["prompt_conv_state"][one].rearrange("l o k c -> (l o k) c"), cso[0:HALO, 2, :]).then_inc(so, 16)
                for g in range(2):
                    pool.dma_start(outs["sample_conv_state"][one, 4 * g:4 * g + 4].rearrange("l b k c -> (l b k) c"), cso[0:4 * HALO, g, :]).then_inc(so, 16)
                def values(it):
                    for b in range(G):
                        for n in range(4):
                            load_page(pool, vpg[:, it % 2, b, n, :], ins["cache_sb_v"], it, b, n, v_loaded[it % 2],
                                      (sm["v_used"], it - 1) if it >= 2 and b == n == 0 else None)
                pool.wait_ge(sm["w_used"], U_OUT)
                values(0)
                values(1)
                pool.wait_ge(sm["st_done"], 16)
                for p_ in range(2):
                    pool.dma_start(outs["sample_gla_state"][one, :, 2 * p_:2 * p_ + 2].rearrange("l b h k v -> (h k) (l b) v"), st[:, :, p_, :]).then_inc(so, 16)
                pool.wait_ge(sm["s2_ready"], 2)
                pool.dma_start(outs["prompt_gla_state"][one].rearrange("l o (p h) k v -> (h k) (l o p) v", p=2), s2[:, :, :]).then_inc(so, 16)
                for it in range(2, ITS):
                    values(it)
                sum_squares(1)
                pool.wait_ge(so, 16 * 10)
                pool.wait_ge(sm["state_loaded"], 16 * 4)
                for v in v_loaded:
                    pool.wait_ge(v, 256 * ITS // 2)
                pool.dma_reset()

            @block.tensor
            def _(pe):
                def product(out, pairs, width=T, m=P):
                    last = None
                    for n, (lh, ll, rh, rl) in enumerate(pairs):
                        pe.matmul(out, lh, rh, start=(n == 0), stop=False)
                        pe.matmul(out, lh, rl, start=False, stop=False)
                        last = pe.matmul(out, ll, rh, start=False, stop=(n == len(pairs) - 1))
                    return last

                def unit(u, out, rhs_h, rhs_l, n, k0=0, tiles=KD, first_wait=None, c8=0, order=None):
                    slot = (u if isinstance(u, int) else u[0]) % SLOTS
                    pe.wait_ge(sm["w_lo"], u + 1 if isinstance(u, int) else u[1] + (u[0] + 1))
                    last = None
                    for i, k in enumerate(order or range(n)):
                        if first_wait is not None:
                            pe.wait_ge(first_wait, c8 + i + 1)
                        f, l_ = k0 + i == 0, k0 + i == tiles - 1
                        kk = k0 + k
                        pe.matmul(out, w_h[:, slot, k, :], rhs_h[:, kk, 0:T], start=f, stop=False)
                        pe.matmul(out, w_h[:, slot, k, :], rhs_l[:, kk, 0:T], start=False, stop=False)
                        last = pe.matmul(out, w_l[:, slot, k, :], rhs_h[:, kk, 0:T], start=False, stop=l_)
                    last.then_inc(sm["w_used"], 1)

                def pre_norm():
                    for j in range(KD):
                        pe.wait_ge(sm["sq_ready"], 8 + j + 1)
                        pe.matmul(bank[6][:, 0:T], cst_("mean_d"), sq[:, j % 2, :], start=(j == 0), stop=(j == KD - 1)).then_inc(sm["sq_used"], 1)

                def post_norm(c):
                    pe.wait_ge(sm["ss_done"], 8 * c + 8)
                    pe.matmul(bank[6][:, 0:T], cst_("mean_d"), ss[:, :], start=True, stop=True).then_inc(sm["post_mean"], 1)

                def ffn(k, U0):
                    c = 2 * k

                    def pair(i, u, peeled):
                        for t in range(2):
                            done = (lambda s: pe.wait_ge(s, k * FT + 2 * i + t - 1)) if not peeled else (
                                (lambda s: pe.wait_ge(s, k * FT)) if k else (lambda s: None))
                            done(sm["gate_r"])
                            unit(u(2 * t), bank[2 * t][:, 0:T], hh, hl, KD,
                                 first_wait=sm["h_lo"] if peeled and t == 0 else None, c8=8 * c)
                            done(sm["gate_up"])
                            unit(u(2 * t + 1), bank[2 * t + 1][:, 0:T], hh, hl, KD)
                            if peeled and t == 0:
                                pe.wait_ge(sm["sx_done"], 8 * k + 8)
                                pe.matmul(bank[6][:, 0:T], cst_("mean_d"), sx[:, :], start=True, stop=True).then_inc(sm["x_mean"], 1)
                    pair(0, lambda j: U0 + j, True)
                    with pe.Fori(1, FT // 2) as i:
                        pair(i, lambda j: (U0 + j, i * 4), False)
                    Ud = U0 + 2 * FT

                    def four(i, u, peeled):
                        for n in range(4):
                            if not peeled or n >= 2:
                                pe.wait_ge(sm["f_ready"], 8 * c + n - 1 + (0 if peeled else 4 * i))
                            for m, (k0, kn_) in enumerate(DOWN):
                                if peeled and n == 0:
                                    pe.wait_ge(sm["gu_lo"], k * FT + k0 + kn_)
                                unit(u(3 * n + m), bank[4 + n % 2][:, 0:T], guh, gul, kn_, k0, FT)
                    four(0, lambda j: Ud + j, True)
                    four(1, lambda j: Ud + 12 + j, False)
                    post_norm(c)

                ffn(0, 0)

                pre_norm()
                pe.wait_ge(sm["state_loaded"], 64)
                for g in range(2):
                    for c in range(2):
                        last = pe.transpose(bank[7][:, (2 * g + c) * 120:(2 * g + c) * 120 + 120],
                                            cst[0:120, g, c * P:(c + 1) * P], cst_("ident", 120, 120))
                last.then_inc(sm["cst_turned"], 1)
                def turn_values(k_):
                    pe.wait_ge(sm["zin_act"], LEVEL0 + 4 - 2 + k_ + 1)
                    if k_ >= 2:
                        pe.wait_ge(sm["v_placed"], 2 * k_ - 2)
                    for n in range(NT):
                        rows = P if n < 2 else TS
                        last = pe.transpose(bank[6 + k_ % 2][0:rows, n * P:(n + 1) * P], fT[:, k_, n * P:n * P + rows], cst_("ident"))
                    last.then_inc(sm["v_turned"], 1)

                def level_products(n_):
                    if n_ == 0:
                        pe.wait_ge(sm["zin_act"], LEVEL0 - 2)
                        pe.wait_ge(sm["loga_x"], 2)
                        pe.wait_ge(sm["cst_placed"], 4)
                    else:
                        pe.wait_ge(sm["qk_ready"], n_)
                    for n in level_tiles(n_):
                        rows = P if n < 2 else TS
                        if n_:
                            pe.wait_ge(sm["att_done"], 2 * (level_turns(n_ - 1) + n + 1))
                        for h in range(H):
                            r, p_ = head(h)
                            q_ = gq if n_ == 0 else qt[:, n_ % 2]
                            k_ = gk if n_ == 0 else kt[:, n_ % 2]
                            last = pe.matmul(bank[2 + 2 * n + h % 2][0:rows, p_ * P:p_ * P + rows],
                                             k_[r, p_, n * P:n * P + rows], q_[r, p_, n * P:n * P + rows],
                                             start=True, stop=True)
                        last.then_inc(sm["qk_used"], 1)

                values_seen = 0
                for m, (what, c, _) in enumerate(UNITS_IN):
                    if m >= 4:
                        before = m - 4 if m < LEVEL0 else m - 2
                        pe.wait_ge(*((sm["zin_dve"], before // 2 + 1) if before < 4 else (sm["zin_act"], before - 1)))
                    unit(U_IN + m, in_bank(m)[:, 0:T], hh, hl, KD, first_wait=sm["h_lo"] if m == 0 else None, c8=8)
                    if m == 10:
                        pe.wait_ge(sm["row_loaded"], 32)
                        pe.wait_ge(sm["zin_act"], 9 - 2)
                        for p_ in range(2):
                            last = pe.matmul(bank[4 + p_][:, 0:T], wa2[:, p_ * P:(p_ + 1) * P], glr[:, :], start=True, stop=True)
                        last.then_inc(sm["loga_pre"], 1)
                    if LEVEL0 <= m < LEVEL0 + 8:
                        level_products(m - LEVEL0)
                    if m and UNITS_IN[m - 1][0] in ("gv", "sv"):
                        turn_values(values_seen)
                        values_seen += 1
                turn_values(values_seen)

                pe.wait_ge(sm["zin_act"], NIN - 2)
                pe.wait_ge(sm["att_done"], 2 * level_turns(8))
                for n in range(NT):
                    rows = P if n < 2 else TS
                    for c in range(2):
                        last = pe.transpose(bank[n // 2][0:rows, (n % 2) * 256 + c * P:(n % 2) * 256 + (c + 1) * P],
                                            ks[:, c, n * P:n * P + rows], cst_("ident"))
                last.then_inc(sm["out_turned"], 1)
                for c in range(2):
                    pe.wait_ge(sm["conv_packed"], c + 1)
                    for g in range(2):
                        pe.transpose(bank[2][0:120, (2 * g + c) * P:(2 * g + c + 1) * P], cst[:, c, g * 120:g * 120 + 120], cst_("ident"))
                    last = pe.transpose(bank[3][0:HALO, c * P:(c + 1) * P], ext[:, c, TP:TP + HALO], cst_("ident"))
                last.then_inc(sm["out_turned"], 1)

                pe.wait_ge(sm["khat_ready"], 2)
                pe.wait_ge(sm["v_placed"], 12)
                for n in range(NT):
                    rows = P if n < 2 else TS
                    for p_ in range(2):
                        last = pe.transpose(bank[6 + n // 2][0:rows, (n % 2) * 256 + p_ * P:(n % 2) * 256 + (p_ + 1) * P],
                                            kt[:, 0, p_, n * P:n * P + rows], cst_("ident"))
                last.then_inc(sm["knat_turned"], 1)

                pe.wait_ge(sm["out_placed_act"], 2)
                pe.wait_ge(sm["out_placed_dve"], 2)
                pe.wait_ge(sm["qb_ready"], 4)
                for g in range(DB // G):
                    for p_ in range(2):
                        for b in range(G):
                            c0 = (G * g + b) * 32
                            last = pe.matmul(bank[0][32 * b:32 * b + 32, TP + g * TS:TP + (g + 1) * TS], qb[:, p_, c0:c0 + 32],
                                             ks[:, p_, TP:T], start=(p_ == 0), stop=(p_ == 1), skip_group_check=True)
                last.then_inc(sm["zn_prod"], 1)
                for h in range(H):
                    r, p_ = head(h)
                    pe.matmul(bank[2 * (h % 2)][:, p_ * P:(p_ + 1) * P], ks[r, p_, P:TP], qs[r, p_, P:TP], start=True, stop=True)
                    last = pe.matmul(bank[2 * (h % 2) + 1][:, p_ * TP:(p_ + 1) * TP], ks[r, p_, 0:P], qs[r, p_, 0:TP], start=True, stop=True)
                last.then_inc(sm["pz_prod"], 1)

                pe.wait_ge(sm["knat_ready"], 2)
                for ch in range(2):
                    for h in range(H):
                        r, p_ = head(h)
                        last = pe.matmul(bank[4 + ch][r, p_ * DV:(p_ + 1) * DV],
                                         kn[:, ch, h * DK:(h + 1) * DK], gv[:, ch, h * DV:(h + 1) * DV], start=True, stop=True)
                    last.then_inc(sm["s1_prod"], 1)

                def gla_outputs(pair):
                    def mm(h, cols, lhs, rhs, first=False, end=False):
                        return pe.matmul(bank[O_BANK[h]][:, cols], lhs, rhs, start=first, stop=end, skip_group_check=True)
                    vh = [slice(h * DV, (h + 1) * DV) for h in range(H)]
                    for h in pair:
                        mm(h, slice(0, P), gv[:, 0, vh[h]], att[:, 0, h, :], True)
                        mm(h, slice(P, TP), gv[:, 1, vh[h]], att[:, 1, h, :])
                        mm(h, slice(TP, T), gv[:, 2, vh[h]], att[:, 2, h, 0:TS])
                    for h in pair:
                        r, p_ = head(h)
                        mm(h, slice(P, TP), s1[r, p_, :], qt[r, 0, p_, P:TP])
                    for b in range(DB):
                        c = slice(TP + DT * b, TP + DT * b + DT)
                        for h in pair:
                            r, p_ = head(h)
                            last = mm(h, c, st[r, b, p_, :], qt[r, 0, p_, c], end=(b == DB - 1))
                            if b == DB - 1:
                                last.then_inc(sm["o_prod"], 1)
                pe.wait_ge(sm["s1_ready"], 1)
                gla_outputs((0, 1))
                pe.wait_ge(sm["pz_sp"], 1)
                pe.wait_ge(sm["zn_neg"], 1)
                for n in range(3):
                    pe.matmul(bank[n][:, :], cst_("from_here"), ps_s[:, n, :], start=True, stop=(n == 0), skip_group_check=True)
                for p_ in range(2):
                    o = bank[1 + p_][:, :].rearrange("p (h t) -> p h t", h=2)[:, :, P:TP]
                    later = ps_s[:, 0, 2 * P * p_:2 * P * (p_ + 1)].rearrange("p (h t) -> p h t", h=2)
                    last = pe.matmul(o, cst_("ones"), later, start=False, stop=True, skip_group_check=True)
                last.then_inc(sm["pz_cum"], 1)
                pe.wait_ge(sm["s2_ready"], 2)
                gla_outputs((2, 3))
                pe.wait_ge(sm["pz_w"], 1)
                for h in range(H):
                    r, p_ = head(h)
                    c0 = p_ * TP
                    pe.matmul(bank[3][r, c0:c0 + TP], svn[:, 0, h * DK:(h + 1) * DK],
                              ps_z[:, 1 + p_, (h % 2) * TP:(h % 2 + 1) * TP], start=True, stop=False, skip_group_check=True)
                    last = pe.matmul(bank[3][r, c0 + P:c0 + TP], svn[:, 1, h * DK:(h + 1) * DK],
                                     ps_z[:, 0, h * P:(h + 1) * P], start=False, stop=True, skip_group_check=True)
                last.then_inc(sm["po_prod"], 1)
                pe.wait_ge(sm["wn_ready"], 1)
                for g in range(DB // G):
                    last = pe.transpose(bank[2][0:TS, g * P:(g + 1) * P], zn[:, g, :], cst_("ident"))
                last.then_inc(sm["wn_turned"], 1)
                for h in range(H):
                    pe.wait_ge(sm["o_sq"], h + 1)
                    if h == 2:
                        pe.wait_ge(sm["wn_placed"], 1)
                    if h == 3:
                        pe.wait_ge(sm["po_done"], 1)
                    pe.matmul(bank[h][:, 0:T], cst_("mean_dv"), osq[:, h, :], start=True, stop=True).then_inc(sm["o_mean"], 1)
                pe.wait_ge(sm["knm_ready"], 1)
                for b in range(DB):
                    if b % 2 == 0:
                        pe.wait_ge(sm["o_done"], b // 2 + 1)
                    for h in range(H):
                        r, p_ = head(h)
                        c0 = (b % 2) * 256 + p_ * DV
                        last = pe.matmul(bank[O_BANK[b // 2]][r, c0:c0 + DV], knm[:, b, h * DK:(h + 1) * DK],
                                         gv[0:TS, 2, h * DV:(h + 1) * DV], start=True, stop=True)
                    if b % 2:
                        last.then_inc(sm["st_prod"], 1)

                def turn_keys(st_i):
                    pe.wait_ge(k_loaded[st_i % 2], P * (st_i // 2 + 1))
                    for b in range(G):
                        if st_i:
                            pe.wait_ge(sm[KT_SEM[b % 2]], 2 * st_i - 1 + b // 2)
                        for p_ in range(2):
                            for j in range(2):
                                last = pe.transpose(bank[b][:, p_ * 256 + j * P:p_ * 256 + (j + 1) * P],
                                                    kpg[:, st_i % 2, b, j, p_ * P:(p_ + 1) * P], cst_("ident"))
                        last.then_inc(sm["kt_turned"], 1)

                def scores(st_i):
                    it = st_i // 2
                    for k_ in KT_SEM:
                        pe.wait_ge(sm[k_], 2 * st_i + 2)
                    if st_i == 0:
                        pe.wait_ge(sm["st_done"], 16)
                    if st_i % 2 == 0 and it >= 2:
                        pe.wait_ge(sm["z_placed"], it - 1)
                    for p_ in range(2):
                        for b in range(G):
                            c0 = (it // (PAGES // 4) * G + b) * 32
                            last = pe.matmul(bank[4 + it % 2][32 * b:32 * b + 32, st_i % 2 * 256:(st_i % 2 + 1) * 256],
                                             qb[:, p_, c0:c0 + 32], kT[:, st_i % 2, b, p_, :],
                                             start=(p_ == 0), stop=(p_ == 1), skip_group_check=True)
                    last.then_inc(sm["kt_used"], 1)

                def keys(it):
                    turn_keys(2 * it)
                    if it:
                        scores(2 * it - 1)
                    turn_keys(2 * it + 1)
                    scores(2 * it)

                def new_values(g):
                    if g:
                        pe.wait_ge(sm["so_done"], 4 * g)
                    pe.matmul(bank[7][:, 0:256], wTn[:, g, :], svn[:, 2, :], start=True, stop=False, skip_group_check=True)

                def values(it):
                    pe.wait_ge(sm["w_ready"], it + 1)
                    if it:
                        pe.wait_ge(sm["wt_placed"], it)
                    for j in range(4):
                        last = pe.transpose(bank[6][:, j * P:(j + 1) * P], w_[:, it % 2, j * P:(j + 1) * P], cst_("ident"))
                    last.then_inc(sm["wt_turned"], 1)
                    pe.wait_ge(sm["wt_placed"], it + 1)
                    pe.wait_ge(v_loaded[it % 2], 256 * (it // 2 + 1))
                    for j in range(4):
                        for b in range(G):
                            last = pe.matmul(bank[7][32 * b:32 * b + 32, 0:256], wT[:, it % 2, j, 32 * b:32 * b + 32],
                                             vpg[:, it % 2, b, j, :], start=False, stop=(j == 3 and it % 4 == 3), skip_group_check=True)
                    last.then_inc(sm["v_used"], 1)

                def outputs(g):
                    pe.wait_ge(sm["oq_placed"], g + 1)
                    for p_ in range(2):
                        last = pe.transpose(bank[7][:, 256 + p_ * P:256 + (p_ + 1) * P], oq[:, p_ * P:(p_ + 1) * P], cst_("ident"))
                    last.then_inc(sm["oq_turned"], 1)

                for it in range(ITS):
                    keys(it)
                    if it == 0:
                        new_values(0)
                    if it == ITS - 1:
                        scores(2 * it + 1)
                        pe.wait_ge(sm["conv_y"], 1)
                        for c in range(2):
                            last = pe.matmul(bank[0][:, 0:T], cst_("mean_ch"), yT[:, c, :], start=(c == 0), stop=(c == 1))
                        last.then_inc(sm["conv_mean"], 1)
                    if it:
                        values(it - 1)
                    if it == 4:
                        outputs(0)
                        new_values(1)
                pe.wait_ge(sm["conv_v"], 2)
                for c in range(2):
                    last = pe.matmul(bank[1][:, 0:T], cst_("mean_ch"), sq[:, c, :], start=(c == 0), stop=(c == 1))
                last.then_inc(sm["conv_var"], 1)
                values(ITS - 1)
                outputs(1)

                pe.wait_ge(sm["so_done"], 8)
                for n in range(KD):
                    if n >= 2:
                        pe.wait_ge(sm["f_ready"], 8 + n - 1)
                    unit(U_OUT + n, bank[4 + n % 2][:, 0:T], hh, hl, KD, first_wait=sm["mix_lo"] if n == 0 else None, order=MIX_ORDER)
                post_norm(1)
                ffn(1, U_FFN2)

            @block.scalar
            def _(act):
                A = Steps(act, sm["act_step"])
                nsa = nc.scalar.activation

                def hi(u, n=8):
                    if isinstance(u, int):
                        if u >= U_END:
                            return
                        slot = u % SLOTS
                        if u >= SLOTS:
                            act.wait_ge(sm["w_used"], u - SLOTS + 1)
                        act.wait_ge(w_loaded[slot], 16 * (u // SLOTS + 1))
                    else:
                        c, v = u
                        slot = c % SLOTS
                        act.wait_ge(sm["w_used"], v + (c - SLOTS + 1))
                        act.wait_ge(w_loaded[slot], v * (16 // SLOTS) + 16 * (c // SLOTS + 1))
                    A(nsa(w_h[:, slot, 0:n, :], raw[:, slot, 0:n, :], ACT.Copy), sm["w_hi"])

                def rsqrt(mean, out, tmp, done):
                    A(nsa(tmp, mean, ACT.Ln, bias=cst_("eps")))
                    A.settle()
                    return A(nsa(out, tmp, ACT.Exp, scale=-0.5), done)

                def exp_ln():
                    act.preload_act_table_set("natural_log_exp_and_others")

                def pre_norm():
                    for j in range(KD):
                        act.wait_ge(sm["x_ready"], j + 1)
                        if j < 2:
                            act.wait_ge(sm["ss_done"], 8)
                        else:
                            act.wait_ge(sm["sq_used"], j - 1)
                        A(nsa(sq[:, j % 2, :], xT[:, j, :], ACT.Square), sm["sq_ready"])
                    act.wait_ge(sm["sq_used"], 8)
                    rsqrt(bank[6][:, 0:T], rs[:, :], rln[:, :], sm["r_ready"])
                    for j in range(KD):
                        act.wait_ge(sm["h_ready"], j + 1)
                        A(nsa(hh[:, j, 0:T], ht[:, j % 2, :], ACT.Copy), sm["h_hi"])

                def scaled(k):
                    c = 2 * k
                    for j in range(KD):
                        if k:
                            act.wait_ge(sm["x_ready"], 8 * (c - 1) + j + 1)
                        A(nsa(hh[:, j, :], xT[:, j, :], ACT.Copy, scale=par[:, 8 * c + j:8 * c + j + 1]), sm["h_hi"])
                        if j >= 2:
                            act.wait_ge(sm["sx_done"], 8 * k + j - 1)
                        elif k:
                            act.wait_ge(sm["ss_done"], 8 * c)
                        A(nsa(sq[:, j % 2, :], xT[:, j, :], ACT.Square), sm["sq_ready"])
                        if k == 0 and j % 2:
                            hi(j // 2)

                def evac_f(c, n, u, i=None, unguarded=False):
                    add = 0 if i is None else 4 * i
                    act.wait_ge(sm["w_used"], u)
                    A(nsa(fT[:, (n if i is None else bass.ds(i * 4 + n, 1)), :].rearrange("p a t -> p (a t)") if i is not None else fT[:, n, :],
                          bank[4 + n % 2][:, 0:T], ACT.Copy), sm["f_ready"])
                    A.settle()
                    if not unguarded:
                        act.wait_ge(sm["ss_done"], 8 * c + n - 1 + add)
                    src = fT[:, n, :] if i is None else fT[:, bass.ds(i * 4 + n, 1), :].rearrange("p a t -> p (a t)")
                    A(nsa(sq[:, n % 2, :], src, ACT.Square), sm["fsq_ready"])

                def post_norm(c):
                    act.wait_ge(sm["post_mean"], c + 1)
                    rsqrt(bank[6][:, 0:T], rs[:, :], rln[:, :], sm["r_ready"])

                def ffn(k, U0):
                    c = 2 * k
                    scaled(k)
                    act.wait_ge(sm["x_mean"], k + 1)
                    rsqrt(bank[6][:, 0:T], rs[:, :], rln[:, :], sm["r_ready"])

                    def pair(i, u, n, peeled):
                        for t in range(2):
                            act.wait_ge(sm["gate_r"], k * FT + t + 1 + 2 * i)
                            if not (peeled and k == 0):
                                act.wait_ge(sm["gate_up"], (k * FT + t - 1 if not peeled else k * FT) + (0 if peeled else 2 * i))
                            A(nsa(sg[:, t, :], gr[:, t, :], ACT.Silu), sm["gate_act"])
                            for m in range(2):
                                x = u(2 * t + m + LEAD)
                                hi(x if not peeled else x[0] + x[1], n[2 * t + m])
                            act.wait_ge(sm["gt_ready"], k * FT + t + 1 + 2 * i)
                            dst = guh[:, t, :] if peeled else guh[:, bass.ds(i * 2 + t, 1), :].rearrange("p a t -> p (a t)")
                            A(nsa(dst, gt[:, t, :], ACT.Copy), sm["gu_hi"])
                    pair(0, lambda j: (U0 + j, 0), [8] * 4, True)
                    per = [(sm["gate_act"], 2), (sm["gu_hi"], 2), (sm["w_hi"], 4)]
                    with A.repeat(1, FT // 2, per) as i:
                        pair(i, lambda j: (U0 + j, i * 4), [8] * 4, False)
                    Ud = U0 + 2 * FT

                    def four(i, last):
                        for n in range(4):
                            for m in range(3):
                                nxt = 12 * i + 3 * n + m + LEAD
                                hi(Ud + nxt, DOWN[nxt % 3][1] if nxt < 24 else 8)
                            evac_f(c, 4 * i + n, Ud + 12 * i + 3 * n + 3, unguarded=(4 * i + n < 2))
                    exp_ln()
                    four(0, False)
                    four(1, k == 1)
                    post_norm(c)

                act.wait_ge(sm["par_ready"], 1)
                exp_ln()
                ffn(0, 0)
                pre_norm()

                act.wait_ge(sm["cst_turned"], 1)
                for g in range(2):
                    for c in range(2):
                        dst = ext[:, c, HALO + TP:].rearrange("p (b t) -> p b t", b=DB)[:, 4 * g:4 * g + 4, 0:HALO]
                        A(nsa(dst, bank[7][:, (2 * g + c) * 120:(2 * g + c + 1) * 120].rearrange("p (b t) -> p b t", b=4), ACT.Copy), sm["cst_placed"])
                def place_values(k_):
                    dst, c0 = (gv, k_ * P) if k_ < 4 else (svn, (k_ - 4) * P)
                    act.wait_ge(sm["v_turned"], k_ + 1)
                    A(nsa(dst[:, 0:2, c0:c0 + P], bank[6 + k_ % 2][:, 0:256].rearrange("p (n c) -> p n c", n=2), ACT.Copy), sm["v_placed"])
                    A(nsa(dst[0:TS, 2, c0:c0 + P], bank[6 + k_ % 2][0:TS, 256:256 + P], ACT.Copy), sm["v_placed"])

                def decays(n_):
                    act.wait_ge(sm["qk_d"], n_)
                    d = dd[:, n_ % 2, :, 0:T if n_ <= 3 else TP]
                    A(nsa(d, d, ACT.Abs))
                    A.settle()
                    A(nsa(d, d, ACT.Exp, scale=-1.0 / 16), sm["qk_e"])

                values_seen = 0
                for m, (what, c, _) in enumerate(UNITS_IN):
                    b_ = in_bank(m)[:, 0:T]
                    if what != "a":
                        act.wait_ge(sm["w_used"], U_IN + m + 1)
                    if what == "g":
                        A(nsa(sq[:, c, :], b_, ACT.Sigmoid), sm["zin_act"])
                    elif what == "gg":
                        A(nsa(gate[:, c, :], b_, ACT.Silu), sm["zin_act"])
                    elif what == "glr":
                        A(nsa(glr[:, :], in_bank(m)[0:16, 0:T], ACT.Copy), sm["zin_act"])
                        exp_ln()
                    elif what == "gk":
                        A(nsa(gk[:, c, :], b_, ACT.Copy), sm["zin_act"])
                    elif what == "sk":
                        A(nsa(ks[:, c, :], b_, ACT.Copy), sm["zin_act"])
                    elif what in ("gv", "sv"):
                        A(nsa(fT[:, c + (4 if what == "sv" else 0), :], b_, ACT.Copy), sm["zin_act"])
                    elif what != "a":
                        A(nsa((gq if what == "gq" else qs)[:, c, :], b_, ACT.Copy, scale=DK ** -0.5), sm["zin_act"])
                    if m + LEAD < NIN:
                        hi(U_IN + m + LEAD)
                    if m == 10:
                        act.wait_ge(sm["loga_pre"], 1)
                        for p_ in range(2):
                            A(nsa(dd[:, 0, p_, :], bank[4 + p_][:, 0:T], ACT.Identity, bias=par[:, PAR["gla_b_a"] + p_:PAR["gla_b_a"] + p_ + 1]), sm["loga_x"])
                    if m == 11:
                        act.wait_ge(sm["loga_neg"], 1)
                        A(nsa(dd[:, 1], dd[:, 1], ACT.Exp))
                        A.settle()
                        A(nsa(dd[:, 1], dd[:, 1], ACT.Ln, bias=1.0), sm["loga_l"])
                    if m == LEVEL0:
                        decays(1)
                        decays(2)
                    elif LEVEL0 < m <= LEVEL0 + 5:
                        decays(m - LEVEL0 + 2)
                    if m and UNITS_IN[m - 1][0] in ("gv", "sv"):
                        place_values(values_seen)
                        values_seen += 1
                place_values(values_seen)
                act.wait_ge(sm["par_ready"], 1)
                act.wait_ge(sm["qb_clear"], 1)
                A.settle()
                for h2 in range(2):
                    r = slice(h2 * DK, (h2 + 1) * DK)
                    for p_ in range(2):
                        dst = qb[r, p_, :].rearrange("p (b h q) -> p b h q", h=H, q=DT)[:, :, 2 * p_ + h2, :]
                        A(nsa(dst, qs[r, p_, TP:T].rearrange("p (b q) -> p b q", q=DT), ACT.Copy), sm["qb_ready"])
                act.wait_ge(sm["out_turned"], 2)
                A(nsa(skn[:, 0:2, :], bank[0][:, :].rearrange("p (n c) -> p n c", n=2), ACT.Copy), sm["out_placed_act"])
                A(nsa(skn[0:TS, 2, :], bank[1][0:TS, 0:256], ACT.Copy), sm["out_placed_act"])

                act.wait_ge(sm["khat_d"], 2)
                A(nsa(dd[:, 0], dd[:, 0], ACT.Exp, scale=1.0 / 16), sm["khat_e"])
                A(nsa(dd[:, 1], bb[:, :, :], ACT.Exp, scale=1.0 / 16), sm["khat_e"])
                A(nsa(aend[:, :, 0:2], bb[:, :, P - 1:TP:P], ACT.Exp, scale=1.0 / 16), sm["khat_e"])
                A(nsa(aend[:, :, 2:10], bb[:, :, TP + DT - 1:T:DT], ACT.Exp, scale=1.0 / 16), sm["khat_e"])
                act.wait_ge(sm["knat_turned"], 1)
                A(nsa(kn[:, 0:2, :], bank[6][:, :].rearrange("p (n c) -> p n c", n=2), ACT.Copy), sm["knat_ready"])
                A(nsa(kn[0:TS, 2, :], bank[7][0:TS, 0:256], ACT.Copy), sm["knat_ready"])
                act.wait_ge(sm["s1_prod"], 1)
                A(nsa(s1[:, :, :].rearrange("p a v -> p (a v)"), bank[4][:, 0:256], ACT.Copy), sm["s1_ready"])
                act.wait_ge(sm["pz_neg"], 1)
                A(nsa(ps_t[:, :, :], ps_t[:, :, :], ACT.Exp))
                A.settle()
                A(nsa(ps_t[:, :, :], ps_t[:, :, :], ACT.Ln, bias=1.0), sm["pz_l"])
                act.wait_ge(sm["zn_neg"], 1)
                A(nsa(tn[:, :, :], tn[:, :, :], ACT.Exp))
                A.settle()
                A(nsa(tn[:, :, :], tn[:, :, :], ACT.Ln, bias=1.0), sm["zn_l"])

                def squares(pair):
                    for h in pair:
                        act.wait_ge(sm["o_prod"], h + 1)
                        A(nsa(osq[:, h, :], bank[O_BANK[h]][:, 0:T], ACT.Square), sm["o_sq"])
                squares((0, 1))
                act.wait_ge(sm["pz_lw"], 3)
                A(nsa(ps_z[:, :, :], ps_z[:, :, :], ACT.Exp), sm["pz_w"])
                act.wait_ge(sm["zn_lw"], 1)
                A(nsa(zn[:, :, :], zn[:, :, :], ACT.Exp), sm["wn_ready"])
                squares((2, 3))
                act.wait_ge(sm["po_prod"], 1)
                A(nsa(fT[:, 4:6, 0:TP], bank[3][:, :].rearrange("p (a t) -> p a t", a=2), ACT.Copy), sm["po_done"])
                act.wait_ge(sm["wn_turned"], 1)
                A(nsa(wTn[0:TS, :, :].rearrange("p g c -> p (g c)"), bank[2][0:TS, 0:256], ACT.Copy), sm["wn_placed"])
                for h in range(H):
                    act.wait_ge(sm["o_mean"], h + 1)
                    rsqrt(bank[h][:, 0:T], osq[:, h, :], rln[:, :], sm["o_r"])
                    A.settle()

                act.wait_ge(sm["o_done"], 4)
                def keys(it):
                    for st_i in (2 * it, 2 * it + 1):
                        for b in (0, 2):
                            act.wait_ge(sm["kt_turned"], 4 * st_i + b + 1)
                            if st_i >= 2:
                                act.wait_ge(sm["kt_used"], st_i - 1)
                            A(nsa(kT[:, st_i % 2, b].rearrange("p a c -> p (a c)"), bank[b][:, :], ACT.Copy), sm["kt_act"])

                def softplus(it):
                    t = t_[:, it % 2, :]
                    act.wait_ge(sm["z_placed"], it + 1)
                    if it >= 2:
                        act.wait_ge(sm["lw_ready"], it - 1)
                    A(nsa(t, z_[:, it % 2, :], ACT.Abs))
                    A.settle()
                    A(nsa(t, t, ACT.Exp, scale=-1.0))
                    A.settle()
                    A(nsa(t, t, ACT.Ln, bias=1.0), sm["z_l"])

                def weights(it):
                    act.wait_ge(sm["lw_ready"], it + 1)
                    if it >= 2:
                        act.wait_ge(sm["wt_turned"], it - 1)
                    A(nsa(w_[:, it % 2, :], z_[:, it % 2, :], ACT.Exp), sm["w_ready"])

                for it in range(ITS):
                    keys(it)
                    if it:
                        weights(it - 1)
                    softplus(it)

                def mix_hi(tiles):
                    for j in tiles:
                        A(nsa(hh[:, j, 0:T], fT[:, j, :], ACT.Copy), sm["mix_hi"])
                act.wait_ge(sm["kt_turned"], 8 * ITS)
                mix_hi(MIX_ORDER[0:4])
                for c in range(2):
                    act.wait_ge(sm["conv_d"], c + 1)
                    A(nsa(sq[:, c, :], yT[:, c, :], ACT.Square), sm["conv_v"])
                weights(ITS - 1)
                act.wait_ge(sm["conv_var"], 1)
                rsqrt(bank[1][:, 0:T], rs[:, :], rln[:, :], sm["conv_r"])
                act.wait_ge(sm["conv_n"], 2)
                for c in range(2):
                    A(nsa(fT[:, 6 + c, :], yT[:, c, :], ACT.Silu, bias=par[:, PAR["conv_norm_b"] + c:PAR["conv_norm_b"] + c + 1]), sm["conv_done"])

                exp_ln()
                A.settle()
                mix_hi(MIX_ORDER[4:6])

                act.wait_ge(sm["v_used"], ITS)
                hi(U_OUT)
                act.wait_ge(sm["so_done"], 8)
                mix_hi(MIX_ORDER[6:8])
                for n in range(1, LEAD):
                    hi(U_OUT + n)
                act.wait_ge(sm["mix_lo"], KD)
                for n in range(KD):
                    hi(U_OUT + n + LEAD)
                    evac_f(1, n, U_OUT + n + 1, unguarded=(n < 2))
                post_norm(1)
                ffn(1, U_FFN2)

            @block.vector
            def _(dve):
                V = Steps(dve, sm["dve_step"])

                def lo(u, n=8):
                    if isinstance(u, int):
                        if u >= U_END:
                            return
                        slot = u % SLOTS
                        dve.wait_ge(sm["w_hi"], u + 1)
                    else:
                        c, v = u
                        slot = c % SLOTS
                        dve.wait_ge(sm["w_hi"], v + (c + 1))
                    V(dve.tensor_tensor(w_l[:, slot, 0:n, :], raw[:, slot, 0:n, :], w_h[:, slot, 0:n, :].bitcast(F32), ALU.subtract), sm["w_lo"])

                def pre_norm():
                    dve.wait_ge(sm["r_ready"], 3)

                    def mul(j):
                        if j >= 2:
                            dve.wait_ge(sm["h_lo"], 8 + j - 1)
                        V(dve.scalar_tensor_tensor(ht[:, j % 2, :], xT[:, j, :], par[:, 8 + j:9 + j], rs[:, :], ALU.mult, ALU.mult), sm["h_ready"])
                    mul(0)
                    for j in range(KD):
                        if j + 1 < KD:
                            mul(j + 1)
                        dve.wait_ge(sm["h_hi"], 8 + j + 1)
                        V(dve.tensor_tensor(hl[:, j, 0:T], ht[:, j % 2, :], hh[:, j, 0:T].bitcast(F32), ALU.subtract), sm["h_lo"])

                def scaled(k, j):
                    g = 16 * k + j
                    dve.wait_ge(sm["h_hi"], 16 * k + j + 1)
                    V(dve.scalar_tensor_tensor(hl[:, j, :], xT[:, j, :], par[:, g:g + 1], hh[:, j, :].bitcast(F32), ALU.mult, ALU.subtract), sm["h_lo"])

                def add_square(c, n):
                    dve.wait_ge(sm["fsq_ready"], 8 * c + n + 1)
                    V.settle()
                    V(dve.tensor_tensor(ss[:, :], ss[:, :], sq[:, n % 2, :], ALU.add), sm["ss_done"])

                def post_norm(c):
                    g0 = 24 + 8 * c
                    dve.wait_ge(sm["r_ready"], 2 * c + 2)

                    def term(j):
                        if j >= 2:
                            dve.wait_ge(sm["x_ready"], 8 * c + j - 1)
                        V(dve.scalar_tensor_tensor(ht[:, j % 2, :], fT[:, j, :], par[:, g0 + j:g0 + j + 1], rs[:, :], ALU.mult, ALU.mult), sm["dve_step"])
                        return V.last
                    done = term(0)
                    for j in range(KD):
                        nxt = term(j + 1) if j + 1 < KD else None
                        dve.wait_ge(*done)
                        V(dve.tensor_tensor(xT[:, j, :], xT[:, j, :], ht[:, j % 2, :], ALU.add), sm["x_ready"])
                        done = nxt
                        if c == 1 and j:
                            scaled(1, j - 1)
                    if c == 1:
                        scaled(1, KD - 1)

                def ffn(k, U0):
                    c = 2 * k
                    V(dve.memset(ss[:, :], 0.0))
                    dve.wait_ge(sm["r_ready"], 2 * c + 1)

                    def pair(i, u, peeled):
                        for t in range(2):
                            x = [u(2 * t + m + LEAD) for m in range(2)]
                            x = [a_ + b_ for a_, b_ in x] if peeled else x
                            c0, v = u(2 * t)
                            dve.wait_ge(sm["w_used"], v + (c0 + 1))
                            if not (peeled and k == 0):
                                dve.wait_ge(sm["gate_act"], k * FT if peeled else k * FT + t - 1 + 2 * i)
                            V(dve.tensor_tensor(gr[:, t, :], bank[2 * t][:, 0:T], rs[:, :], ALU.mult), sm["gate_r"])
                            lo(x[0])
                            c0, v = u(2 * t + 1)
                            dve.wait_ge(sm["w_used"], v + (c0 + 1))
                            dve.wait_ge(sm["gate_act"], k * FT + t + 1 + 2 * i)
                            if not (peeled and k == 0):
                                dve.wait_ge(sm["gu_lo"], k * FT if peeled else k * FT + t - 1 + 2 * i)
                            V(dve.tensor_tensor(gt[:, t, :], sg[:, t, :], bank[2 * t + 1][:, 0:T], ALU.mult), sm["gate_up"])
                            V.settle()
                            V(dve.tensor_tensor(gt[:, t, :], gt[:, t, :], rs[:, :], ALU.mult), sm["gt_ready"])
                            lo(x[1])
                            dve.wait_ge(sm["gu_hi"], k * FT + t + 1 + 2 * i)
                            if peeled:
                                d, h_ = gul[:, t, :], guh[:, t, :]
                            else:
                                f = bass.ds(i * 2 + t, 1)
                                d, h_ = (g[:, f, :].rearrange("p a t -> p (a t)") for g in (gul, guh))
                            V(dve.tensor_tensor(d, gt[:, t, :], h_.bitcast(F32), ALU.subtract), sm["gu_lo"])
                    pair(0, lambda j: (U0 + j, 0), True)
                    with V.repeat(1, FT // 2, [(sm["gate_r"], 2), (sm["gate_up"], 2), (sm["gt_ready"], 2), (sm["gu_lo"], 2), (sm["w_lo"], 4)]) as i:
                        pair(i, lambda j: (U0 + j, i * 4), False)
                    Ud = U0 + 2 * FT
                    for i in range(2):
                        for n in range(4):
                            for m in range(3):
                                nxt = 12 * i + 3 * n + m + LEAD
                                lo(Ud + nxt, DOWN[nxt % 3][1] if nxt < 24 else 8)
                            add_square(c, 4 * i + n)
                    post_norm(c)

                V(dve.tensor_copy(par[:, :], par_all[:, one, :].rearrange("p l c -> p (l c)")), sm["par_ready"])
                V.settle()
                for j in range(KD):
                    scaled(0, j)
                    if j % 2:
                        lo(j // 2)
                ffn(0, 0)
                pre_norm()

                dve.wait_ge(sm["w_used"], U_IN)
                V(dve.memset(qb[:, :, :], 0.0), sm["qb_clear"])
                V(dve.memset(gv[TS:P, 2, :], 0.0))
                V(dve.memset(svn[TS:P, 2, :], 0.0))
                for c in range(2):
                    V(dve.memset(ext[:, c, 0:HALO], 0.0))
                V(dve.memset(wTn[:, :, :], 0.0))
                V(dve.memset(att[:, :, :, :], 0.0))
                V(dve.memset(qt[:, :, :, :], 0.0))
                V(dve.memset(kt[:, :, :, :], 0.0))

                def conv(k):
                    V.settle()
                    for c in range(2):
                        w = par[:, PAR["conv_w"] + 2 * k + c:PAR["conv_w"] + 2 * k + c + 1]
                        bias = par[:, PAR["conv_b"] + c:PAR["conv_b"] + c + 1]
                        v = ext[:, c, HALO + TP:].rearrange("p (b t) -> p b t", b=DB)[:, :, k:k + DT]
                        for n, (out, x) in enumerate(((yT[:, c, 0:TP], ext[:, c, k:k + TP]),
                                       (yT[:, c, TP:T].rearrange("p (b t) -> p b t", b=DB), v))):
                            if k == 0:
                                V(dve.tensor_scalar(out, x, w, bias, ALU.mult, ALU.add))
                            else:
                                V(dve.scalar_tensor_tensor(out, x, w, out, ALU.mult, ALU.add),
                                  sm["conv_y"] if k == TAPS - 1 and c == n == 1 else None)

                def blocks(t, w, half=None):
                    if w <= 4:
                        v = t.rearrange("p a (n t) -> p (a n) t", t=2 * w)
                        return v if half is None else v[:, :, half * w:half * w + w]
                    v = t[:, :, 0:TP].rearrange("p a (n t) -> p a n t", t=2 * w)
                    return v if half is None else v[:, :, :, half * w:half * w + w]

                def decay(n_):
                    w = LEVELS[n_ - 1]
                    x = blocks(bb[:, :, :], w)
                    ref = x[:, :, w - 1:w] if w <= 4 else x[:, :, :, w - 1:w]
                    V.settle()
                    V(dve.tensor_tensor(blocks(dd[:, n_ % 2], w), x, ref.to_broadcast(x.shape), ALU.subtract), sm["qk_d"])

                def scale(n_):
                    w = LEVELS[n_ - 1]
                    i = n_ % 2
                    dve.wait_ge(sm["qk_e"], n_)
                    if n_ >= 3:
                        dve.wait_ge(sm["qk_used"], level_turns(n_ - 1))
                    V(dve.tensor_tensor(blocks(qt[:, i], w, 1), blocks(gq[:, :, :], w, 1), blocks(dd[:, i], w, 1), ALU.mult))
                    V(dve.tensor_tensor(blocks(kt[:, i], w, 0), blocks(gk[:, :, :], w, 0), blocks(dd[:, i], w, 0), ALU.mult), sm["qk_ready"])

                def place(n_):
                    for i, n in enumerate(level_tiles(n_)):
                        rows = P if n < 2 else TS
                        dve.wait_ge(sm["qk_used"], level_turns(n_) + i + 1)
                        V.settle()
                        for h2 in range(2):
                            scores = bank[2 + 2 * n + h2][0:rows, 0:2 * P].rearrange("p (h t) -> p h t", h=2)
                            V(dve.copy_predicated(att[0:rows, n, h2::2, 0:rows],
                                                  level[0:rows, n_:n_ + 1, 0:rows].to_broadcast([rows, 2, rows]),
                                                  scores[:, :, 0:rows]), sm["att_done"])
                def level_operands(n_):
                    if n_ == 0:
                        decay(1)
                        decay(2)
                    else:
                        scale(n_)
                        if n_ + 2 < 8:
                            decay(n_ + 2)
                g_seen = 0
                for m, (what, c, _) in enumerate(UNITS_IN):
                    if 4 <= m < 4 + EARLY_TAPS:
                        conv(m - 4)
                    if LEVEL0 <= m < LEVEL0 + 8:
                        level_operands(m - LEVEL0)
                    if LEVEL0 < m <= LEVEL0 + 8:
                        place(m - LEVEL0 - 1)
                    if m + LEAD < NIN:
                        lo(U_IN + m + LEAD)
                    if what == "g":
                        g_seen += 1
                        dve.wait_ge(sm["zin_act"], g_seen)
                        dve.wait_ge(sm["cst_placed"], 4)
                        a_ = bank[(m - 1) % 4]
                        V(dve.tensor_tensor(ext[:, c, HALO:HALO + TP], a_[:, 0:TP], sq[:, c, 0:TP], ALU.mult))
                        V(dve.tensor_tensor(ext[:, c, HALO + TP:].rearrange("p (b t) -> p b t", b=DB)[:, :, HALO:],
                                            a_[:, TP:T].rearrange("p (b t) -> p b t", b=DB),
                                            sq[:, c, TP:T].rearrange("p (b t) -> p b t", b=DB), ALU.mult), sm["zin_dve"])
                        V.settle()
                        V(dve.tensor_copy(cst[:, c, 0:DB * HALO].rearrange("p (b t) -> p b t", b=DB),
                                          ext[:, c, HALO + TP:].rearrange("p (b t) -> p b t", b=DB)[:, :, DT:]), sm["conv_packed"])
                    if m == 10:
                        dve.wait_ge(sm["loga_x"], 2)
                        V(dve.scalar_tensor_tensor(dd[:, 1], dd[:, 0], -1.0, dd[:, 0], ALU.mult, ALU.min), sm["loga_neg"])
                    if m == 12:
                        dve.wait_ge(sm["loga_l"], 1)
                        V(dve.scalar_tensor_tensor(dd[:, 0], dd[:, 0], 0.0, dd[:, 1], ALU.min, ALU.subtract))
                        V.settle()
                        for p_ in range(2):
                            V(dve.tensor_tensor_scan(bb[:, p_, :], cst_("gla_keep"), dd[:, 0, p_, :], 0.0, ALU.mult, ALU.add), sm["b_ready"])
                dve.wait_ge(sm["out_turned"], 2)
                V(dve.tensor_copy(cso[0:4 * HALO, 0:2, :], bank[2][0:4 * HALO, :].rearrange("p (g c) -> p g c", g=2)), sm["out_placed_dve"])
                V(dve.tensor_copy(cso[0:HALO, 2, :], bank[3][0:HALO, 0:256]), sm["out_placed_dve"])

                V.settle()
                for d, x in ((dd[:, 0, :, 0:TP], bb[:, :, 0:TP]), (dd[:, 0, :, TP:T], bb[:, :, TP:T])):
                    n = P if x.shape[2] == TP else DT
                    x = x.rearrange("p a (n t) -> p a n t", t=n)
                    V(dve.tensor_tensor(d.rearrange("p a (n t) -> p a n t", t=n), x[:, :, :, n - 1:n].to_broadcast(x.shape), x, ALU.subtract), sm["khat_d"])
                dve.wait_ge(sm["khat_e"], 4)
                V(dve.tensor_tensor(kt[:, 0], gk[:, :, :], dd[:, 0], ALU.mult), sm["khat_ready"])
                V(dve.tensor_tensor(qt[:, 0], gq[:, :, :], dd[:, 1], ALU.mult), sm["khat_ready"])
                dve.wait_ge(sm["pz_prod"], 1)
                for h in range(H):
                    bias = sbb[:, h:h + 1]
                    V(dve.scalar_tensor_tensor(ps_z[:, 0, h * P:(h + 1) * P], bank[2 * (h % 2)][:, h // 2 * P:(h // 2 + 1) * P], bias, cst_("causal"), ALU.add, ALU.add))
                    c0 = (h % 2) * TP
                    o, i = ps_z[:, 1 + h // 2, c0:c0 + TP], bank[2 * (h % 2) + 1][:, h // 2 * TP:(h // 2 + 1) * TP]
                    V(dve.scalar_tensor_tensor(o[:, 0:P], i[:, 0:P], bias, cst_("causal"), ALU.add, ALU.add))
                    V(dve.tensor_scalar(o[:, P:TP], i[:, P:TP], bias, None, ALU.add))
                V.settle()
                V(dve.scalar_tensor_tensor(ps_t[:, :, :], ps_z[:, :, :], -1.0, ps_z[:, :, :], ALU.mult, ALU.min), sm["pz_neg"])
                dve.wait_ge(sm["zn_prod"], 1)
                V(dve.tensor_tensor(tn[:, 0, 0:H], cst_("head_of"), sbb[:, :], ALU.mult))
                V.settle()
                V(dve.tensor_reduce(bq[:, :], tn[:, 0, 0:H], mybir.AxisListType.X, ALU.add))
                V.settle()
                V(dve.scalar_tensor_tensor(zn[:, :, :].rearrange("p g c -> p (g c)"), bank[0][:, TP:TP + 2 * TS], bq[:, :], cst_("new_mask"), ALU.add, ALU.add))
                V.settle()
                V(dve.scalar_tensor_tensor(tn[:, :, :], zn[:, :, :], -1.0, zn[:, :, :], ALU.mult, ALU.min), sm["zn_neg"])
                dve.wait_ge(sm["s1_ready"], 1)
                dve.wait_ge(sm["s1_prod"], 2)
                for p_ in range(2):
                    V(dve.scalar_tensor_tensor(s2[:, p_, :], s1[:, p_, :], aend[:, p_, 1:2], bank[5][:, p_ * DV:(p_ + 1) * DV], ALU.mult, ALU.add), sm["s2_ready"])
                dve.wait_ge(sm["pz_l"], 1)
                V(dve.scalar_tensor_tensor(ps_s[:, :, :], ps_z[:, :, :], 0.0, ps_t[:, :, :], ALU.max, ALU.add), sm["pz_sp"])
                dve.wait_ge(sm["zn_l"], 1)
                V(dve.scalar_tensor_tensor(tn[:, :, :], zn[:, :, :], 0.0, tn[:, :, :], ALU.max, ALU.add))
                V.settle()
                for g in range(DB // G):
                    V(dve.tensor_tensor_scan(sn[:, g, ::-1], cst_("ones", cols=TS), tn[:, g, ::-1], 0.0, ALU.mult, ALU.add))
                V.settle()
                V(dve.tensor_tensor(zn[:, :, :], zn[:, :, :], sn[:, :, :], ALU.subtract), sm["zn_lw"])
                dve.wait_ge(sm["pz_cum"], 1)
                for n in range(3):
                    V(dve.tensor_tensor(ps_z[:, n, :], ps_z[:, n, :], bank[n][:, :], ALU.subtract), sm["pz_lw"])

                V(dve.tensor_tensor(knm[:, :, :], kn[0:TS, 2:3, :].to_broadcast([TS, DB, 256]),
                                    cst_("batch_of", TS).unsqueeze(2).to_broadcast([TS, DB, 256]), ALU.mult), sm["knm_ready"])

                for h in range(H):
                    dve.wait_ge(sm["o_r"], h + 1)
                    V(dve.scalar_tensor_tensor(fT[:, h, :], bank[O_BANK[h]][:, 0:T], par[:, PAR["gla_norm"] + h:PAR["gla_norm"] + h + 1], osq[:, h, :], ALU.mult, ALU.mult))
                    V.settle()
                    V(dve.tensor_tensor(fT[:, h, :], fT[:, h, :], gate[:, h, :], ALU.mult), sm["o_done"])
                for b in range(DB):
                    if b % 2 == 0:
                        dve.wait_ge(sm["st_prod"], b // 2 + 1)
                    for p_ in range(2):
                        c0 = (b % 2) * 256 + p_ * DV
                        V(dve.scalar_tensor_tensor(st[:, b, p_, :], st[:, b, p_, :], aend[:, p_, 2 + b:3 + b], bank[O_BANK[b // 2]][:, c0:c0 + DV], ALU.mult, ALU.add), sm["st_done"])


                def keys(it):
                    for st_i in (2 * it, 2 * it + 1):
                        for b in (1, 3):
                            dve.wait_ge(sm["kt_turned"], 4 * st_i + b + 1)
                            if st_i >= 2:
                                dve.wait_ge(sm["kt_used"], st_i - 1)
                            V(dve.tensor_copy(kT[:, st_i % 2, b].rearrange("p a c -> p (a c)"), bank[b][:, :]), sm["kt_dve"])
                            k = EARLY_TAPS + 4 * it + st_i % 2 * 2 + b // 2
                            if k < TAPS:
                                conv(k)

                def place_scores(it):
                    dve.wait_ge(sm["kt_used"], 2 * it + 2)
                    if it >= 2:
                        dve.wait_ge(sm["w_ready"], it - 1)
                    V(dve.tensor_scalar(z_[:, it % 2, :], bank[4 + it % 2][:, :], bq[:, :], None, ALU.add), sm["z_placed"])

                def log_weights(it):
                    z, t, s = z_[:, it % 2, :], t_[:, it % 2, :], s_[:, it % 2, :]
                    dve.wait_ge(sm["z_l"], it + 1)
                    V(dve.scalar_tensor_tensor(t, z, 0.0, t, ALU.max, ALU.add))
                    V.settle()
                    later = sn[:, it // 4, 0:1] if it % 4 == 0 else s_[:, 1 - it % 2, 0:1]
                    V(dve.tensor_tensor_scan(s[:, ::-1], cst_("ones", cols=1).to_broadcast([P, 512]), t[:, ::-1], later, ALU.mult, ALU.add))
                    V.settle()
                    V(dve.tensor_tensor(z, z, s, ALU.subtract), sm["lw_ready"])

                def weights(it):
                    dve.wait_ge(sm["wt_turned"], it + 1)
                    if it >= 2:
                        dve.wait_ge(sm["v_used"], it - 1)
                    V(dve.tensor_copy(wT[:, it % 2].rearrange("p n c -> p (n c)"), bank[6][:, :]), sm["wt_placed"])

                def outputs(g):
                    dve.wait_ge(sm["v_used"], 4 * g + 4)
                    if g:
                        dve.wait_ge(sm["oq_turned"], g)
                    V(dve.tensor_copy(oq[:, :], bank[7][:, 0:256]), sm["oq_placed"])
                    dve.wait_ge(sm["oq_turned"], g + 1)
                    for p_ in range(2):
                        for h2 in range(2):
                            r = slice(h2 * DK, (h2 + 1) * DK)
                            c0 = TP + 32 * g
                            src = bank[7][r, 256 + p_ * P:256 + (p_ + 1) * P].rearrange("p (b h q) -> p b h q", h=H, q=DT)[:, :, 2 * p_ + h2, :]
                            V(dve.tensor_copy(fT[r, 4 + p_, c0:c0 + 32].rearrange("p (b q) -> p b q", q=DT), src), sm["so_done"])

                for it in range(ITS):
                    keys(it)
                    if it:
                        weights(it - 1)
                    if it == 4:
                        outputs(0)
                    place_scores(it)
                    log_weights(it)
                dve.wait_ge(sm["conv_mean"], 1)
                for c in range(2):
                    V(dve.tensor_tensor(yT[:, c, :], yT[:, c, :], bank[0][:, 0:T], ALU.subtract), sm["conv_d"])
                weights(ITS - 1)
                dve.wait_ge(sm["conv_r"], 1)
                for c in range(2):
                    g = PAR["conv_norm_g"] + c
                    V(dve.scalar_tensor_tensor(yT[:, c, :], yT[:, c, :], par[:, g:g + 1], rs[:, :], ALU.mult, ALU.mult), sm["conv_n"])

                def mix_lo(first, stop):
                    for i in range(first, stop):
                        j = MIX_ORDER[i]
                        dve.wait_ge(sm["mix_hi"], i + 1)
                        V(dve.tensor_tensor(hl[:, j, 0:T], fT[:, j, :], hh[:, j, 0:T].bitcast(F32), ALU.subtract), sm["mix_lo"])
                mix_lo(0, 6)
                outputs(1)

                lo(U_OUT)
                dve.wait_ge(sm["po_done"], 1)
                V.settle()
                mix_lo(6, KD)
                for n in range(1, LEAD):
                    lo(U_OUT + n)
                V(dve.memset(ss[:, :], 0.0))
                for n in range(KD):
                    lo(U_OUT + n + LEAD)
                    add_square(1, n)
                post_norm(1)
                ffn(1, U_FFN2)

        clear()

    with nc.Block() as block:
        @block.tensor
        def _(pe):
            for n in range(NT):
                rows = P if n < 2 else TS
                for g in range(2):
                    for j in range(4):
                        last = pe.transpose(bank[2 * n + g][0:rows, j * P:(j + 1) * P], xT[:, 4 * g + j, n * P:n * P + rows], cst_("ident"))
                    last.then_inc(sm["y_turned"], 1)

        @block.vector
        def _(dve):
            for n in range(NT):
                rows = P if n < 2 else TS
                for g in range(2):
                    dve.wait_ge(sm["y_turned"], 2 * n + g + 1)
                    dve.tensor_copy(xn[0:rows, n, g * 512:(g + 1) * 512], bank[2 * n + g][0:rows, :]).then_inc(sm["y_placed"], 1)

        @block.sync
        def _(sp_):
            for n in range(2):
                sp_.wait_ge(sm["y_placed"], 2 * n + 2)
                sp_.dma_start(outs["y_prompt"][0, n * P:(n + 1) * P, :], xn[:, n, :]).then_inc(sm["x_stored"], 16)
            sp_.wait_ge(sm["y_placed"], 6)
            sp_.dma_start(outs["y_sample"].rearrange("b t d -> (b t) d"), xn[0:TS, 2, :]).then_inc(sm["x_stored"], 16)
            sp_.wait_ge(sm["x_stored"], 48)
    stack.close()


MIX_ORDER = (0, 1, 2, 3, 6, 7, 4, 5)
O_BANK = (6, 7, 4, 5)
KT_SEM = ("kt_act", "kt_dve")


def head(h):
    return slice((h % 2) * DK, (h % 2 + 1) * DK), h // 2


def level_turns(n_):
    return sum(len(level_tiles(i)) for i in range(n_))


def level_tiles(n_):
    return range(NT if n_ <= 3 else 2)


ITS = DB // G * (PAGES // 4)


def first_page(it):
    return PAGES - 4 - it % (PAGES // 4) * 4


_INS = ["x_prompt", "x_sample", "cache_sb_k", "cache_sb_v", "page_table", "state_gla", "state_conv", "ffn1_norm_pre",
        "ffn1_norm_post", "ffn1_w_gate", "ffn1_w_up", "ffn1_w_down", "mix_norm_pre", "mix_norm_post", "w_in", "gla_w_a2",
        "gla_b_a", "gla_norm", "sb_bias", "conv_w", "conv_b", "conv_norm_g", "conv_norm_b", "w_out", "ffn2_norm_pre",
        "ffn2_norm_post", "ffn2_w_gate", "ffn2_w_up", "ffn2_w_down"]
_OUTS = [("y_prompt", (1, TP, D)), ("y_sample", (DB, DT, D)), ("prompt_sb_k", (L, 1, TP, H, DK)),
         ("prompt_sb_v", (L, 1, TP, H, DK)), ("prompt_gla_state", (L, 1, H, DK, DV)),
         ("prompt_conv_state", (L, 1, HALO, 256)), ("sample_sb_k", (L, DB, DT, H, DK)),
         ("sample_sb_v", (L, DB, DT, H, DK)), ("sample_gla_state", (L, DB, H, DK, DV)),
         ("sample_conv_state", (L, DB, HALO, 256))]


def kernel(**inputs):
    import concourse.bacc as bacc
    from concourse.bass_utils import run_bass_kernel_spmd

    nc = bacc.Bacc("TRN2", target_bir_lowering=False, num_devices=1)
    arrays = {f"in_{name}": np.ascontiguousarray(inputs[name]) for name in _INS}
    arrays["in_const"], arrays["in_level"] = CONST, LEVEL
    ins = {name[3:]: nc.dram_tensor(name, a.shape, mybir.dt.from_np(a.dtype), kind="ExternalInput").ap()
           for name, a in arrays.items()}
    outs = {name: nc.dram_tensor(f"out_{name}", shape, F32, kind="ExternalOutput").ap() for name, shape in _OUTS}
    build(nc, ins, outs)
    r = run_bass_kernel_spmd(nc, [arrays], core_ids=[0])
    return tuple(r.results[0][f"out_{name}"] for name, _ in _OUTS)
```
